# Optimizing a Trainium2 kernel written in Bass

```python
import jax, jax.numpy as jnp
from jax import lax
import numpy as np

D_MODEL = 1024
BATCH = 1
SEQ = 512
DEPTH = 4
DEC_BATCH = 8
DEC_SEQ = 1
PAST_LEN = 1024
PAGE_SIZE = 128

N_MIXERS = 3
N_A = (DEPTH + 2) // N_MIXERS
N_B = (DEPTH + 1) // N_MIXERS
N_C = DEPTH // N_MIXERS
SC_WIDTH = 3
HEAD_DIM = 64
N_HEADS = D_MODEL // HEAD_DIM
Q_BLOCK = 128
FORGET_BIAS_INIT = 2.0
MASK_VALUE = -1e30
LRU_WIDTH = ((4 * D_MODEL) // 3) // 128 * 128
LRU_BLOCKS = 16
LRU_BLOCK = LRU_WIDTH // LRU_BLOCKS
LRU_CONV = 4
LRU_C = 8.0
D_FF = ((8 * D_MODEL) // 3 + 127) // 128 * 128
FFN_CONV = 3
EPS = 1e-6

kernel_name = 'fox_shortconv_rglru_hybrid_step'

def rmsnorm(x, g):
    xf = x.astype(jnp.float32)
    y = xf * lax.rsqrt(jnp.mean(xf * xf, axis=-1, keepdims=True) + EPS)
    return (y * g.astype(jnp.float32)).astype(x.dtype)

def causal_dwconv(u, buf, w, b=None):
    width = w.shape[0]
    t = u.shape[1]
    ext = jnp.concatenate([buf.astype(u.dtype), u], axis=1)
    y = w[0] * ext[:, :t]
    for k in range(1, width):
        y = y + w[k] * ext[:, k:k + t]
    if b is not None:
        y = y + b
    return y, ext[:, t:]

def short_conv_mixer(xn, buf, w_in, conv_w, w_out):
    b_gate, c_gate, h = jnp.split(xn @ w_in, 3, axis=-1)
    y, new_buf = causal_dwconv(c_gate * h, buf, conv_w)
    return (b_gate * y) @ w_out, new_buf

def fox_project(xn, w_qkv, w_f, b_f, q_norm, k_norm):
    bsz, t, _ = xn.shape
    q, k, v = jnp.split(xn @ w_qkv, 3, axis=-1)
    q = rmsnorm(q.reshape(bsz, t, N_HEADS, HEAD_DIM), q_norm)
    k = rmsnorm(k.reshape(bsz, t, N_HEADS, HEAD_DIM), k_norm)
    v = v.reshape(bsz, t, N_HEADS, HEAD_DIM)
    log_f = jax.nn.log_sigmoid((xn @ w_f + b_f).astype(jnp.float32))
    return q, k, v, log_f

def fox_attention(q, c_q, q_pos, segments):
    bsz, tq, h, dh = q.shape
    qb = Q_BLOCK if tq % Q_BLOCK == 0 else tq
    nb = tq // qb
    scale = dh ** -0.5
    q_blocks = q.reshape(bsz, nb, qb, h, dh).swapaxes(0, 1)
    cq_blocks = c_q.reshape(bsz, nb, qb, h).swapaxes(0, 1)
    pos_blocks = q_pos.reshape(nb, qb)
    sizes = [seg[0].shape[1] for seg in segments]

    def one_block(args):
        qblk, cqblk, pblk = args
        logits = []
        for k, _, c_k, k_pos in segments:
            s = jnp.einsum('bqhd,bkhd->bhqk', qblk, k).astype(jnp.float32) * scale
            s = s + cqblk.transpose(0, 2, 1)[..., None] - c_k.transpose(0, 2, 1)[:, :, None, :]
            logits.append(jnp.where(k_pos[None, :] <= pblk[:, None], s, MASK_VALUE))
        p = jax.nn.softmax(jnp.concatenate(logits, axis=-1), axis=-1)
        out = None
        offset = 0
        for (_, v, _, _), n in zip(segments, sizes):
            part = jnp.einsum('bhqk,bkhd->bqhd', p[..., offset:offset + n].astype(v.dtype), v)
            out = part if out is None else out + part
            offset += n
        return out

    out = lax.map(one_block, (q_blocks, cq_blocks, pos_blocks))
    return out.swapaxes(0, 1).reshape(bsz, tq, h * dh)

def _lru_combine(left, right):
    a_l, b_l = left
    a_r, b_r = right
    return a_l * a_r, a_r * b_l + b_r

def rglru_mixer(xn, h0, buf, w_in, b_in, conv_w, conv_b, w_a, b_a, w_i, b_i, lam, w_out):
    gate, xb = jnp.split(xn @ w_in + b_in, 2, axis=-1)
    gate = jax.nn.gelu(gate)
    xb, new_buf = causal_dwconv(xb, buf, conv_w, conv_b)
    bsz, t, _ = xb.shape
    xblk = xb.reshape(bsz, t, LRU_BLOCKS, LRU_BLOCK)
    r = jax.nn.sigmoid(jnp.einsum('btnc,ncd->btnd', xblk, w_a).reshape(bsz, t, LRU_WIDTH) + b_a)
    i = jax.nn.sigmoid(jnp.einsum('btnc,ncd->btnd', xblk, w_i).reshape(bsz, t, LRU_WIDTH) + b_i)
    log_a = -LRU_C * r.astype(jnp.float32) * jax.nn.softplus(-lam.astype(jnp.float32))
    a = jnp.exp(log_a)
    bterm = jnp.sqrt(-jnp.expm1(2.0 * log_a)) * (i * xb).astype(jnp.float32)
    bterm = bterm.at[:, 0].add(a[:, 0] * h0.astype(jnp.float32))
    _, hs = lax.associative_scan(_lru_combine, (a, bterm), axis=1)
    y = (hs.astype(xn.dtype) * gate) @ w_out
    return y, hs[:, -1].astype(xn.dtype), new_buf

def conv_ffn(xn, buf, w_gate, w_up, conv_w, conv_b, w_down):
    g, new_buf = causal_dwconv(xn @ w_gate, buf, conv_w, conv_b)
    return (jax.nn.silu(g) * (xn @ w_up)) @ w_down, new_buf

def setup_inputs(seed: int = 0) -> dict:
    key = jax.random.key(seed)
    keys = iter(jax.random.split(key, 48))

    def nrm(shape, scale=1.0):
        return jax.random.normal(next(keys), shape, jnp.float32) * scale

    n_pages = PAST_LEN // PAGE_SIZE
    n_used = DEC_BATCH * n_pages
    n_pool = n_used + n_used // 4
    d = D_MODEL

    x_prompt = nrm((BATCH, SEQ, d))
    x_sample = nrm((DEC_BATCH, DEC_SEQ, d))
    state_sconv = nrm((N_A, DEC_BATCH, SC_WIDTH - 1, d))
    cache_k = nrm((N_B, n_pool, PAGE_SIZE, N_HEADS, HEAD_DIM))
    cache_v = nrm((N_B, n_pool, PAGE_SIZE, N_HEADS, HEAD_DIM))
    cache_logf = jax.nn.log_sigmoid(FORGET_BIAS_INIT + nrm((N_B, n_pool, PAGE_SIZE, N_HEADS)))
    page_table = jax.random.permutation(next(keys), n_pool)[:n_used].reshape(DEC_BATCH, n_pages).astype(jnp.int32)
    state_lru_h = nrm((N_C, DEC_BATCH, LRU_WIDTH), 0.5)
    state_lru_conv = nrm((N_C, DEC_BATCH, LRU_CONV - 1, LRU_WIDTH))
    state_ffn_conv = nrm((DEPTH, DEC_BATCH, FFN_CONV - 1, D_FF))

    a0 = jax.random.uniform(next(keys), (N_C, LRU_WIDTH), jnp.float32, 0.9, 0.999)
    s0 = a0 ** (1.0 / LRU_C)
    lru_lambda = jnp.log(s0) - jnp.log1p(-s0)

    return {
        'x_prompt': x_prompt,
        'x_sample': x_sample,
        'state_sconv': state_sconv,
        'cache_k': cache_k,
        'cache_v': cache_v,
        'cache_logf': cache_logf,
        'page_table': page_table,
        'state_lru_h': state_lru_h,
        'state_lru_conv': state_lru_conv,
        'state_ffn_conv': state_ffn_conv,
        'mix_norm': 1.0 + nrm((DEPTH, d), 0.1),
        'ffn_norm': 1.0 + nrm((DEPTH, d), 0.1),
        'sc_w_in': nrm((N_A, d, 3 * d), d ** -0.5),
        'sc_conv_w': nrm((N_A, SC_WIDTH, d), SC_WIDTH ** -0.5),
        'sc_w_out': nrm((N_A, d, d), d ** -0.5),
        'fox_w_qkv': nrm((N_B, d, 3 * d), d ** -0.5),
        'fox_w_f': nrm((N_B, d, N_HEADS), d ** -0.5),
        'fox_b_f': FORGET_BIAS_INIT + nrm((N_B, N_HEADS), 0.1),
        'fox_q_norm': 1.0 + nrm((N_B, HEAD_DIM), 0.1),
        'fox_k_norm': 1.0 + nrm((N_B, HEAD_DIM), 0.1),
        'fox_w_o': nrm((N_B, d, d), d ** -0.5),
        'lru_w_in': nrm((N_C, d, 2 * LRU_WIDTH), d ** -0.5),
        'lru_b_in': nrm((N_C, 2 * LRU_WIDTH), 0.02),
        'lru_conv_w': nrm((N_C, LRU_CONV, LRU_WIDTH), LRU_CONV ** -0.5),
        'lru_conv_b': nrm((N_C, LRU_WIDTH), 0.02),
        'lru_w_a': nrm((N_C, LRU_BLOCKS, LRU_BLOCK, LRU_BLOCK), LRU_BLOCK ** -0.5),
        'lru_b_a': nrm((N_C, LRU_WIDTH), 0.02),
        'lru_w_i': nrm((N_C, LRU_BLOCKS, LRU_BLOCK, LRU_BLOCK), LRU_BLOCK ** -0.5),
        'lru_b_i': nrm((N_C, LRU_WIDTH), 0.02),
        'lru_lambda': lru_lambda,
        'lru_w_out': nrm((N_C, LRU_WIDTH, d), LRU_WIDTH ** -0.5),
        'ffn_w_gate': nrm((DEPTH, d, D_FF), d ** -0.5),
        'ffn_w_up': nrm((DEPTH, d, D_FF), d ** -0.5),
        'ffn_conv_w': nrm((DEPTH, FFN_CONV, D_FF), FFN_CONV ** -0.5),
        'ffn_conv_b': nrm((DEPTH, D_FF), 0.02),
        'ffn_w_down': nrm((DEPTH, D_FF, d), D_FF ** -0.5),
    }

def reference(x_prompt, x_sample, state_sconv, cache_k, cache_v, cache_logf, page_table,
              state_lru_h, state_lru_conv, state_ffn_conv,
              mix_norm, ffn_norm, sc_w_in, sc_conv_w, sc_w_out,
              fox_w_qkv, fox_w_f, fox_b_f, fox_q_norm, fox_k_norm, fox_w_o,
              lru_w_in, lru_b_in, lru_conv_w, lru_conv_b, lru_w_a, lru_b_a, lru_w_i, lru_b_i,
              lru_lambda, lru_w_out,
              ffn_w_gate, ffn_w_up, ffn_conv_w, ffn_conv_b, ffn_w_down):
    n_pages = PAST_LEN // PAGE_SIZE
    past = n_pages * PAGE_SIZE
    xp, xs = x_prompt, x_sample
    bp, tp = xp.shape[:2]
    bs, ts = xs.shape[:2]
    pos_p = jnp.arange(tp, dtype=jnp.int32)
    pos_past = jnp.arange(past, dtype=jnp.int32)
    pos_new = past + jnp.arange(ts, dtype=jnp.int32)

    sc_p, sc_s = [], []
    k_p, v_p, lf_p, k_s, v_s, lf_s = [], [], [], [], [], []
    lh_p, lh_s, lc_p, lc_s = [], [], [], []
    fc_p, fc_s = [], []

    for i in range(DEPTH):
        j = i // N_MIXERS
        hp = rmsnorm(xp, mix_norm[i])
        hs = rmsnorm(xs, mix_norm[i])
        if i % N_MIXERS == 0:
            zero_buf = jnp.zeros((bp, SC_WIDTH - 1, D_MODEL), hp.dtype)
            yp, nbp = short_conv_mixer(hp, zero_buf, sc_w_in[j], sc_conv_w[j], sc_w_out[j])
            ys, nbs = short_conv_mixer(hs, state_sconv[j], sc_w_in[j], sc_conv_w[j], sc_w_out[j])
            sc_p.append(nbp)
            sc_s.append(nbs)
        elif i % N_MIXERS == 1:
            qp, kp, vp, lfp = fox_project(hp, fox_w_qkv[j], fox_w_f[j], fox_b_f[j], fox_q_norm[j], fox_k_norm[j])
            cp = jnp.cumsum(lfp, axis=1)
            yp = fox_attention(qp, cp, pos_p, ((kp, vp, cp, pos_p),)) @ fox_w_o[j]
            qs, ks, vs, lfs = fox_project(hs, fox_w_qkv[j], fox_w_f[j], fox_b_f[j], fox_q_norm[j], fox_k_norm[j])
            k_past = cache_k[j, page_table].reshape(bs, past, N_HEADS, HEAD_DIM)
            v_past = cache_v[j, page_table].reshape(bs, past, N_HEADS, HEAD_DIM)
            lf_past = cache_logf[j, page_table].reshape(bs, past, N_HEADS).astype(jnp.float32)
            c_past = jnp.cumsum(lf_past, axis=1)
            c_new = c_past[:, -1:] + jnp.cumsum(lfs, axis=1)
            ys = fox_attention(qs, c_new, pos_new,
                               ((k_past, v_past, c_past, pos_past), (ks, vs, c_new, pos_new))) @ fox_w_o[j]
            k_p.append(kp)
            v_p.append(vp)
            lf_p.append(lfp)
            k_s.append(ks)
            v_s.append(vs)
            lf_s.append(lfs)
        else:
            h_zero = jnp.zeros((bp, LRU_WIDTH), hp.dtype)
            c_zero = jnp.zeros((bp, LRU_CONV - 1, LRU_WIDTH), hp.dtype)
            yp, nhp, ncp = rglru_mixer(hp, h_zero, c_zero, lru_w_in[j], lru_b_in[j], lru_conv_w[j], lru_conv_b[j],
                                       lru_w_a[j], lru_b_a[j], lru_w_i[j], lru_b_i[j], lru_lambda[j], lru_w_out[j])
            ys, nhs, ncs = rglru_mixer(hs, state_lru_h[j], state_lru_conv[j], lru_w_in[j], lru_b_in[j], lru_conv_w[j],
                                       lru_conv_b[j], lru_w_a[j], lru_b_a[j], lru_w_i[j], lru_b_i[j], lru_lambda[j],
                                       lru_w_out[j])
            lh_p.append(nhp)
            lh_s.append(nhs)
            lc_p.append(ncp)
            lc_s.append(ncs)
        xp = xp + yp
        xs = xs + ys

        hp = rmsnorm(xp, ffn_norm[i])
        hs = rmsnorm(xs, ffn_norm[i])
        zero_ffn = jnp.zeros((bp, FFN_CONV - 1, D_FF), hp.dtype)
        yp, nfp = conv_ffn(hp, zero_ffn, ffn_w_gate[i], ffn_w_up[i], ffn_conv_w[i], ffn_conv_b[i], ffn_w_down[i])
        ys, nfs = conv_ffn(hs, state_ffn_conv[i], ffn_w_gate[i], ffn_w_up[i], ffn_conv_w[i], ffn_conv_b[i], ffn_w_down[i])
        fc_p.append(nfp)
        fc_s.append(nfs)
        xp = xp + yp
        xs = xs + ys

    new_sconv_prompt = jnp.stack(sc_p)
    new_sconv_sample = jnp.stack(sc_s)
    new_k_prompt = jnp.stack(k_p)
    new_v_prompt = jnp.stack(v_p)
    new_logf_prompt = jnp.stack(lf_p)
    new_k_sample = jnp.stack(k_s)
    new_v_sample = jnp.stack(v_s)
    new_logf_sample = jnp.stack(lf_s)
    new_lru_h_prompt = jnp.stack(lh_p)
    new_lru_h_sample = jnp.stack(lh_s)
    new_lru_conv_prompt = jnp.stack(lc_p)
    new_lru_conv_sample = jnp.stack(lc_s)
    new_ffn_conv_prompt = jnp.stack(fc_p)
    new_ffn_conv_sample = jnp.stack(fc_s)
    return (xp, xs,
            new_sconv_prompt, new_sconv_sample,
            new_k_prompt, new_v_prompt, new_logf_prompt,
            new_k_sample, new_v_sample, new_logf_sample,
            new_lru_h_prompt, new_lru_h_sample,
            new_lru_conv_prompt, new_lru_conv_sample,
            new_ffn_conv_prompt, new_ffn_conv_sample)


_drawn_inputs = setup_inputs


def setup_inputs(seed=0):
    import zlib

    import numpy as np

    out = dict(_drawn_inputs(seed))
    spreads = {}
    factors = {'lru_b_a': 8.0, 'lru_b_i': 7.623, 'ffn_conv_b': 3.115}
    for name, (base, spread) in spreads.items():
        noise = np.random.default_rng([zlib.crc32(name.encode()), seed]).standard_normal(out[name].shape)
        drawn = base * np.exp(spread * noise) if base else spread * noise
        out[name] = __import__('jax').numpy.asarray(drawn.astype(out[name].dtype))
    for name, factor in factors.items():
        out[name] = (out[name] * factor).astype(out[name].dtype)
    return out
```

```python
from contextlib import ExitStack

import concourse.bass as bass
from concourse import mybir

P = 128
F32 = mybir.dt.float32
F32R = mybir.dt.float32r
I32 = mybir.dt.int32
ALU = mybir.AluOpType
ACT = mybir.ActivationFunctionType
AX = mybir.AxisListType
ds = bass.ds

EPS = 1e-6
LRU_C = 8.0
MASK_VALUE = -1e30
NS = 8
HD = 64


def hybrid_step(nc, I, O):
    D = I["x_prompt"].shape[2]
    SEQ = I["x_prompt"].shape[1]
    T = SEQ + NS
    TH = T // 2
    DC = D // P
    FF = I["ffn_w_gate"].shape[2]
    FC = FF // P
    KH = FC // 2
    LW = I["lru_w_out"].shape[1]
    LC = LW // P
    LB = I["lru_w_a"].shape[2]
    NBLK = I["lru_w_a"].shape[1]
    NH = D // HD
    NPG = I["page_table"].shape[1]
    NPOOL = I["cache_k"].shape[1]
    DEPTH = I["mix_norm"].shape[0]
    QB = SEQ // P
    assert T % 4 == 0 and P * 5 == LB * 8 and LC == 10 and FC % 2 == 0 and DC == 8 and NH == 16

    class Seg:
        pass

    segs, order = {}, []
    nu = ng = 0
    for name, units, kt, upg in (
            [("c0", 8, 8, 1), ("h0", 8, 8, 1), ("b0", 8, 8, 1), ("so0", 8, 8, 1), ("gu0", 2 * FC, 8, 1), ("dn0", 16, KH, 2),
             ("q", 8, 8, 1), ("k", 8, 8, 1), ("v", 8, 8, 1), ("wo", 8, 8, 1), ("gu1", 2 * FC, 8, 1), ("dn1", 16, KH, 2),
             ("lg", LC, 8, 1), ("lx", LC, 8, 1), ("gates", 0, 0, 1), ("lo", 8, LC, 1), ("gu2", 2 * FC, 8, 1), ("dn2", 16, KH, 2),
             ("c1", 8, 8, 1), ("h1", 8, 8, 1), ("b1", 8, 8, 1), ("so1", 8, 8, 1), ("gu3", 2 * FC, 8, 1), ("dn3", 16, KH, 2)]):
        s = Seg()
        s.name, s.units, s.kt, s.u0, s.g0 = name, units, kt, nu, ng
        nu += units
        ng += units // upg if units else 2 * LC
        s.halves = units // 2
        segs[name] = s
        if units:
            order.append(s)
    for a, b in zip(order, order[1:] + [None]):
        a.next_kt = b.kt if b else None

    def gsrc(name):
        j = int(name[-1]) if name[-1].isdigit() else 0
        W = {"c": (I["sc_w_in"], D), "h": (I["sc_w_in"], 2 * D), "b": (I["sc_w_in"], 0), "so": (I["sc_w_out"], 0),
             "q": (I["fox_w_qkv"], 0), "k": (I["fox_w_qkv"], D), "v": (I["fox_w_qkv"], 2 * D), "wo": (I["fox_w_o"], 0),
             "lg": (I["lru_w_in"], 0), "lx": (I["lru_w_in"], LW), "lo": (I["lru_w_out"], 0), "dn": (I["ffn_w_down"], 0)}
        w, c = W[name.rstrip("0123")]
        return w[j].rearrange("(k p) n -> p k n", p=P), c

    rows = {}
    nrows = 0
    plan = []
    for name in ("mix_norm", "ffn_norm", "sc_conv_w", "state_sconv", "ffn_conv_w", "ffn_conv_b", "state_ffn_conv",
                 "lru_b_in", "lru_conv_w", "lru_conv_b", "lru_b_a", "lru_b_i", "lru_lambda", "state_lru_h",
                 "state_lru_conv"):
        ap = I[name]
        n = 1
        for d in ap.shape:
            n *= d
        n //= P
        rows[name] = nrows
        dims = " ".join(f"d{i}" for i in range(len(ap.shape)))
        flat = ap.rearrange(f"{dims} -> ({dims})").rearrange("(r p) -> r p", p=P)
        at = 0
        while at < n:
            take = min(n - at, P - (nrows + at) % P)
            plan.append(((nrows + at) // P, (nrows + at) % P, take, flat[at:at + take, :]))
            at += take
        nrows += n
    NBK = -(-nrows // P)

    at = [16512]

    def place(name, shape, dt, offset=None):
        size = 4
        for d in shape[1:]:
            size *= d
        if offset is None:
            offset = at[0]
            at[0] += -(-size // 32) * 32
        return nc.alloc_sbuf_tensor_at(name, shape, dt, offset=offset)

    SLOT = 4 * T
    x = place("x", [P, DC, T], F32)
    XG = at[0]
    xh = place("xh", [P, DC, T], F32R)
    xl = place("xl", [P, DC, T], F32R)
    wraw = place("wraw", [P, 2, KH, P], F32)
    whi = place("whi", [P, 2, KH, P], F32R)
    wlo = place("wlo", [P, 2, KH, P], F32R)
    WORK = at[0]
    hh = place("hh", [P, FC, T], F32R)
    hl = place("hl", [P, FC, T], F32R)
    par = place("par", [P, nrows], F32)
    TMP = at[0]
    ext = place("ext", [P, T + 4], F32)
    rstd = place("rstd", [P, T], F32)
    acc = place("acc", [P, T], F32)
    tt = place("tt", [P, T], F32)
    ty = place("ty", [P, T], F32)
    tsl = place("tsl", [P, T], F32)
    tsq = place("tsq", [P, T], F32)
    tz = place("tz", [P, T], F32)
    ident = place("ident", [P, P], F32)
    ones = place("ones", [P, P], F32)
    blk = place("blk", [P, P], F32)
    sto = place("sto", [P, 11 * FC], F32)
    sadd = place("sadd", [P, FC, NS], F32)
    stmp = place("stmp", [P, FC, NS], F32)
    eps = place("eps", [P, 1], F32)
    pt = place("pt", [1, NS * NPG], I32)
    bf = place("bf", [NH, 1], F32)
    qg = place("qg", [P, 1], F32)
    kg = place("kg", [P, 1], F32)
    jsel = place("jsel", [P, 4], F32)
    vsr = place("vsr", [NS, D], F32)
    identr = place("identr", [P, P], F32R)
    maskr = place("maskr", [P, P], F32R)
    pick = place("pick", [P, NH], F32R)
    wf = place("wf", [P, DC, NH], F32)
    tri = place("tri", [P, P], F32)
    assert at[0] <= 229368, at[0]

    def slot(name, first, n, dt=F32):
        return place(name, [P, n, T], dt, WORK + first * SLOT)

    par_st = place("par_st", [P, NBK, P], F32, WORK)
    x_st = place("x_st", [P, QB, D], F32, WORK + 12288)
    xs_st = place("xs_st", [NS, D], F32, WORK + 12288 + 16384)
    rst = place("rst", [P, 2, P], F32, TMP)
    sqb = slot("sqb", 0, 8)
    cst = slot("cst", 8, 8)
    qT = slot("qT", 8, 8)
    kT = slot("kT", 30, 8)
    vtok = [place("v01", [P, 2, D], F32, WORK + 18 * SLOT), place("v23", [P, 2, D], F32, WORK + 40 * SLOT)]
    sc = place("sc", [P, NS * NPG, NH], F32, WORK + 16 * SLOT)
    lfb = place("lfb", [P, NS * NPG, NH], F32, WORK + 38 * SLOT)
    pages = place("pages", [P, 4, D], F32, XG + DC * SLOT)
    qb = place("qb", [P, 2, D], F32, XG)
    ztok = place("ztok", [P, D], F32, XG + 8192)
    kst = place("kst", [P, D], F32, XG + 12288)
    kss = place("kss", [NS, D], F32, WORK + 0 * SLOT)
    negc = place("negc", [P, SEQ], F32R, TMP)
    nmax = place("nmax", [P, QB * NH], F32, TMP + 3 * SLOT + 32)
    rsum = place("rsum", [P, QB * NH], F32, TMP + 3 * SLOT + 32 + 256)
    rinv = place("rinv", [P, NH], F32, TMP + 3 * SLOT + 32 + 512)
    lftok = place("lftok", [P, QB + 1, NH], F32, TMP + 3 * SLOT + 32 + 640)
    smal = place("smal", [P, 2, P], F32, TMP + 3 * SLOT + 32 + 960)
    osb = place("osb", [P, D], F32, TMP + 4 * SLOT + 32)
    sm = place("sm", [P, 6, P], F32, TMP + 6 * SLOT + 32)
    lfT = place("lfT", [NH, T], F32, TMP + 7 * SLOT + 32)
    gate = slot("gate", 0, LC)
    la = slot("la", LC, LC)
    xc = slot("xc", 22, LC)
    lb = slot("lb", 22 + LC, LC)
    bandA = place("bandA", [P, LC, 3 * P], F32, XG)
    bandI = place("bandI", [P, LC, 3 * P], F32, XG + LC * 3 * P * 4)
    lsp = place("lsp", [P, 8, LC], F32, WORK + 20 * SLOT)
    hst = place("hst", [P, 9, LC], F32, WORK + 20 * SLOT + 512)
    y_st = place("y_st", [P, 2, D], F32, WORK)

    psum = ExitStack()
    lin = [psum.enter_context(nc.psum_tensor(f"lin{i}", [P, 2, 512], F32)) for i in range(2)]
    aux = psum.enter_context(nc.psum_tensor("aux", [P, 2, 512], F32))
    aux2 = psum.enter_context(nc.psum_tensor("aux2", [P, 2, 512], F32))

    def sems(names):
        return [psum.enter_context(nc.semaphore(n)) for n in names.split()]

    raw_landed = sems("raw_landed0 raw_landed1")
    hi_ready, lo_ready, unit_done, out_free = sems("hi_ready lo_ready unit_done out_free")
    x_landed, par_landed, small_landed, consts = sems("x_landed par_landed small_landed consts")
    filled, fill_free, x_in, copies = sems("filled fill_free x_in copies")
    xh_ready, xg_ready, sq_ready, acc_ready = sems("xh_ready xg_ready sq_ready acc_ready")
    ssq_ready, root_ready, rstd_ready = sems("ssq_ready root_ready rstd_ready")
    pad_zero, sadd_ready, sadd_step, y_ready = sems("pad_zero sadd_ready sadd_step y_ready")
    ffn_tap, sc_tap, lru_tap, conv_ready, state_kept = sems("ffn_tap sc_tap lru_tap conv_ready state_kept")
    silu_ready, scaled_ready, c_scaled, conv_scaled = sems("silu_ready scaled_ready c_scaled conv_scaled")
    z_hi, z_lo = sems("z_hi z_lo")
    rows_T, rows_copied, rows_out = sems("rows_T rows_copied rows_out")
    head_sq, head_sum, head_root, head_recip, normed = sems("head_sq head_sum head_root head_recip normed")
    v_T, v_copied, v_out, k_out = sems("v_T v_copied v_out k_out")
    lf_pe, lf_act, lf_dve, lf_rows, lf_landed, lf_out = sems("lf_pe lf_act lf_dve lf_rows lf_landed lf_out")
    suffix, suffix_in = sems("suffix suffix_in")
    s_ready, max_ready, exp_ready = sems("s_ready max_ready exp_ready")
    pT_ready, pT_copied, pv_done = sems("pT_ready pT_copied pv_done")
    zt_step, zt_ready, zT_hi = sems("zt_step zt_ready zT_hi")
    b67_filled, b67_free, qb_ready = sems("b67_filled b67_free qb_ready")
    page_landed = sems("page0 page1 page2 page3")
    k_mult, k_reduced, v_used, v_sum = sems("k_mult k_reduced v_used v_sum")
    sm_dve, sm_pe, sm_act = sems("sm_dve sm_pe sm_act")
    osb_zero, osb_ready, o_T, o_hi, zs_ready = sems("osb_zero osb_ready o_T o_hi zs_ready")
    lsp_act, lsp_dve, gelu_ready, xb_ready = sems("lsp_act lsp_dve gelu_ready xb_ready")
    band_zero, band_landed, gate_ready, lru_ix = sems("band_zero band_landed gate_ready lru_ix")
    lru_th, lru_ex, lru_q, lru_root = sems("lru_th lru_ex lru_q lru_root")
    lru_b, lru_h, lru_zt, h_kept = sems("lru_b lru_h lru_zt h_kept")
    yT_ready, yT_copied = sems("yT_ready yT_copied")
    y_out = sems("y_out0 y_out1")
    block = psum.enter_context(nc.Block())

    def above_zero(value):
        return not isinstance(value, int) or value > 0

    def pair(ap):
        return ap[:, :, 0:TH]

    def two(ap):
        if len(ap.shape) == 3:
            return ap.rearrange("p o (a b) -> p (o a) b", a=2)
        return ap.rearrange("p (a b) -> p a b", a=2)

    def at1(tile, m):
        return tile[:, ds(m, 1), :]

    def col(name, off):
        return par[:, ds(rows[name] + off, 1)]

    def loop(e, n, body, peel_first=True, peel_last=True):
        a = 1 if peel_first else 0
        b = n - 1 if peel_last else n
        if peel_first:
            body(0, True, False)
        if b - a > 1:
            with e.Fori(a, b) as i:
                body(i, False, False)
        elif b - a == 1:
            body(a, False, False)
        if peel_last:
            body(n - 1, False, True)

    conv0 = {}
    n_ = 0
    for name, k in (("sc0", DC), ("ffn0", FC), ("ffn1", FC), ("lru", LC), ("ffn2", FC), ("sc1", DC), ("ffn3", FC)):
        conv0[name] = n_
        n_ += k
    NORMS = 2 * DEPTH

    def gcol(n, m):
        return col("ffn_norm" if n % 2 else "mix_norm", (n // 2) * DC + m)

    OUTP = {"so0": 1, "dn0": 2, "wo": 3, "dn1": 4, "lo": 5, "dn2": 6, "so1": 7, "dn3": 8}

    B67 = [(0, "qb", 0), (2, "ko", 0), (4, "ko", 1), (6, "qb", 1), (8, "ko", 2), (10, "ko", 3), (12, "ko", 4), (14, "qb", 2),
           (20, "zT", 0), (22, "qb", 3), (30, "qb", 4), (36, "zT", 1), (38, "qb", 5), (46, "qb", 6), (52, "zT", 2),
           (54, "qb", 7), (66, "zT", 3)]
    STEPS = QB * NH

    def b67_before(n):
        if n == 0:
            return b67_free, 0
        kinds = [k for _, k, _ in B67[:n]]
        q = kinds.count("qb")
        return (qb_ready, q) if kinds[-1] == "qb" else (b67_free, n - q)
    kv = [(b, h) for b in range(QB) for h in range(NH)]
    pt_ring = [tsq, tz]
    p_ring = [ty, tsl]
    psf = {"S": [lin[0][:, 0, :], lin[0][:, 1, :]], "PT": [lin[1][:, 0, :], lin[1][:, 1, :]]}

    def flat2(ps):
        return ps[:, :, :].rearrange("p a b -> p (a b)")

    def state_rows(kind, j):
        if kind == "ffn":
            q = FC * 5
            pr = O["new_ffn_conv_prompt"][j].rearrange("b r (c p) -> (b r c) p", p=P)
            sm_ = O["new_ffn_conv_sample"][j].rearrange("s r (c p) -> s r c p", p=P)
            moves = [(pr, 0, 0, 2 * FC)]
            moves += [(sm_[s, 1], (2 + s) // 5, ((2 + s) % 5) * FC, FC) for s in range(NS)]
            return [q, q], moves
        if kind == "sc":
            pr = O["new_sconv_prompt"][j].rearrange("b r (c p) -> (b r c) p", p=P)
            sm_ = O["new_sconv_sample"][j].rearrange("s r (c p) -> s r c p", p=P)
            return [10 * DC], [(pr, 0, 0, 2 * DC)] + [(sm_[s, 1], 0, (2 + s) * DC, DC) for s in range(NS)]
        pr = O["new_lru_conv_prompt"][j].rearrange("b r (c p) -> (b r c) p", p=P)
        sm_ = O["new_lru_conv_sample"][j].rearrange("s r (c p) -> s r c p", p=P)
        return [11 * LC], [(pr, 0, 0, 3 * LC)] + [(sm_[s, 2], 0, (3 + s) * LC, LC) for s in range(NS)]

    STATES = [("sc", 0), ("ffn", 0), ("ffn", 1), ("lru", 0), ("ffn", 2), ("sc", 1), ("ffn", 3)]
    states_of = {"b0": 0, "dn0": 1, "dn1": 2, "lo": 3, "dn2": 4, "b1": 5, "dn3": 6}
    rows_dmas = [0]
    for kind, j in STATES:
        rows_dmas.append(rows_dmas[-1] + len(state_rows(kind, j)[1]))

    pieces = []
    for b in range(8):
        r = LB * b
        while r < LB * (b + 1):
            n = min(LB * (b + 1), (r // P + 1) * P) - r
            pieces.append((r // P, r % P, b, r - LB * b, n))
            r += n

    def sources(m):
        cc, g = m % 5, m // 5
        lo = LB * (P * cc // LB)
        hi = LB * -(-P * (cc + 1) // LB)
        return [5 * g + c for c in range(lo // P, -(-hi // P))]

    @block.sync
    def _(sp):
        def load(seg, it, p):
            u = seg.u0 + 2 * it + p
            if above_zero(u - 1):
                sp.wait_ge(lo_ready, u - 1)
            name = seg.name
            if name.startswith("gu"):
                w = I["ffn_w_up" if p else "ffn_w_gate"][int(name[2])].rearrange("(k p) n -> p k n", p=P)
                src = w[:, :, ds(it * P, P)]
            elif name.startswith("dn"):
                w = I["ffn_w_down"][int(name[2])].rearrange("(k p) n -> p k n", p=P)
                src = w[:, p * KH:(p + 1) * KH, ds(it * P, P)]
            else:
                w, c0 = gsrc(name)
                src = w[:, :, ds(it * 2 * P + (c0 + p * P), P)]
            sp.dma_start(wraw[:, p, 0:seg.kt, :], src).then_inc(raw_landed[p], 16)

        def body(seg):
            def f(it, first, last):
                load(seg, it, 0)
                load(seg, it, 1)
            return f

        def page(cache, pt_index, slot_, free=None, uses=0):
            idx = sp.value_load(pt[0:1, ds(pt_index, 1)], min_val=0, max_val=NPOOL - 1)
            if free:
                sp.wait_ge(free, uses)
            sp.dma_start(pages[:, slot_:slot_ + 1, :], cache[0][ds(idx, 1)].rearrange("a p h d -> p a (h d)")
                         ).then_inc(page_landed[slot_], 16)

        for seg in order:
            if seg.name == "wo":
                body(seg)(0, True, False)
                sp.wait_ge(small_landed, 16 * 8)
                sp.wait_ge(unit_done, segs["v"].u0 + 8)
                for g in range(4):
                    page(I["cache_k"], g, g)
                with sp.Fori(1, NS * NPG // 4) as i:
                    for g in range(4):
                        page(I["cache_k"], 4 * i + g, g, k_reduced, 4 * i + (g - 3))
                sp.wait_ge(k_reduced, NS * NPG)
                for g in range(4):
                    page(I["cache_v"], g * NPG, g)
                with sp.Fori(1, NPG) as i:
                    for g in range(4):
                        page(I["cache_v"], i + g * NPG, g, v_used, 4 * i + (g - 3))
                with sp.Fori(0, NPG) as i:
                    for g in range(4):
                        page(I["cache_v"], i + (4 + g) * NPG, g, v_used, 4 * i + (4 * NPG + g - 3))
                with sp.Fori(1, seg.halves) as i:
                    body(seg)(i, False, False)
            elif seg.name == "lo":
                body(seg)(0, True, False)
                sp.wait_ge(band_zero, 2)
                for band, w in ((bandA, I["lru_w_a"]), (bandI, I["lru_w_i"])):
                    for cc, r0, b, br, n in pieces:
                        off = LB * b - P * (cc - 1)
                        for g in range(2):
                            sp.dma_start(band[r0:r0 + n, 5 * g + cc, off:off + LB],
                                         w[0, 8 * g + b, br:br + n, :]).then_inc(band_landed, 16)
                with sp.Fori(1, seg.halves) as i:
                    body(seg)(i, False, False)
            else:
                loop(sp, seg.halves, body(seg), peel_first=seg.u0 == 0, peel_last=False)

    @block.tensor
    def _(pe):
        mm = nc.tensor.matmul

        def unit(u, p, kt, ps, g, rhs_h, rhs_l, k0, start, stop, ready):
            pe.wait_ge(lo_ready, u + 1)
            if start:
                if above_zero(g - 1):
                    pe.wait_ge(out_free, g - 1)
            for k in range(kt):
                ready(k0 + k)
                for w, r in ((whi, rhs_h), (whi, rhs_l), (wlo, rhs_h)):
                    for half in range(2):
                        last = mm(ps[:, half, 0:TH], w[:, p, k, :], r[:, k0 + k, half * TH:(half + 1) * TH],
                                  start=start and k == 0 and w is whi and r is rhs_h,
                                  stop=stop and k == kt - 1 and w is wlo)
            last.then_inc(unit_done, 1)

        def norm_sum(n):
            pe.wait_ge(acc_ready, 9 * n + 9)
            for half in range(2):
                last = mm(aux[:, half, 0:TH], ones[:, :], acc[:, half * TH:(half + 1) * TH], start=True, stop=True)
            last.then_inc(ssq_ready, 1)

        def state_T(j):
            kind, lay = STATES[j]
            widths, _ = state_rows(kind, lay)
            name = {"sc": f"sc{lay}", "ffn": f"ffn{lay}", "lru": "lru"}[kind]
            pe.wait_ge(state_kept, conv0[name] + {"sc": DC, "ffn": FC, "lru": LC}[kind])
            for i, w in enumerate(widths):
                last = nc.tensor.transpose(aux2[0:w, i, 0:P], sto[:, i * w:(i + 1) * w], ident[:, :])
            if kind == "lru":
                pe.wait_ge(h_kept, LC)
                last = nc.tensor.transpose(aux2[0:9 * LC, 1, 0:P], hst[:, :, :].rearrange("p q c -> p (q c)"), ident[:, :])
            last.then_inc(rows_T, 1)

        def project(seg, norm=None, ready=None, extra=None):
            rh, rl = (xh, xl) if ready is None else (hh, hl)
            n_in = None if ready else norm_of(seg)

            def normed_input(k):
                pe.wait_ge(xg_ready, DC * n_in + k + 1)
            rd = ready or normed_input

            def body(it, first, last):
                for p in range(2):
                    u = seg.u0 + 2 * it + p
                    unit(u, p, seg.kt, lin[p], seg.g0 + 2 * it + p, rh, rl, 0, True, True, rd)
                    if first and p == 0 and norm is not None:
                        norm_sum(norm)
                    if first and p == 0 and seg.name in states_of and seg.name != "b0" and seg.name != "b1":
                        state_T(states_of[seg.name])
                    if extra:
                        extra(2 * it + p, first and p == 0)
                if first and seg.name in ("b0", "b1"):
                    state_T(states_of[seg.name])
            loop(pe, seg.halves, body, peel_last=False)

        def norm_of(seg):
            return {"c0": 0, "h0": 0, "b0": 0, "gu0": 1, "q": 2, "k": 2, "v": 2, "gu1": 3, "lg": 4, "lx": 4, "gu2": 5,
                    "c1": 6, "h1": 6, "b1": 6, "gu3": 7}[seg.name]

        def down(l):
            seg = segs[f"dn{l}"]
            z0 = conv0[f"ffn{l}"]

            def rd(k):
                if k == 0:
                    pe.wait_ge(z_lo, z0 + KH)
                elif k == KH:
                    pe.wait_ge(z_lo, z0 + FC)

            def body(i2, first, last):
                for a in range(2):
                    for p in range(2):
                        u = seg.u0 + 4 * i2 + 2 * a + p
                        unit(u, p, KH, lin[a], seg.g0 + 2 * i2 + a, hh, hl, p * KH, p == 0, p == 1, rd)
                    if first and a == 0:
                        state_T(states_of[seg.name])
            loop(pe, DC // 2, body, peel_last=False)

        fills = [("par", f) for f in range(-(-NBK // 4))] + [("xs", 0)] + [("x", c) for c in range(DC)]
        nsmall = len(fills) - DC
        pe.wait_ge(consts, 1)
        pe.wait_ge(par_landed, 16 * len(plan))
        for i, (what, j) in enumerate(fills):
            bank = (aux, aux2)[(i % 4) // 2][:, i % 2, :]
            if i >= 4:
                if i - 4 < nsmall:
                    pe.wait_ge(fill_free, i - 3)
                else:
                    pe.wait_ge(x_in, i - 3 - nsmall)
            if what == "xs":
                pe.wait_ge(x_landed, 32)
            if what == "par":
                for b in range(4 * j, min(4 * j + 4, NBK)):
                    n = min(P, nrows - b * P)
                    last = nc.tensor.transpose(bank[:, (b % 4) * P:(b % 4) * P + n], par_st[0:n, b, :], ident[0:n, 0:n])
            elif what == "xs":
                for c in range(DC):
                    last = nc.tensor.transpose(bank[:, c * NS:(c + 1) * NS], xs_st[:, c * P:(c + 1) * P], ident[0:NS, 0:NS])
            else:
                for t in range(QB):
                    last = nc.tensor.transpose(bank[:, t * P:(t + 1) * P], x_st[:, t, j * P:(j + 1) * P], ident[:, :])
            last.then_inc(filled, 1)

        def short_conv(j, n):
            project(segs[f"c{j}"], norm=n)
            project(segs[f"h{j}"])
            project(segs[f"b{j}"])
            project(segs[f"so{j}"], ready=lambda k: pe.wait_ge(z_lo, conv0[f"sc{j}"] + k + 1))

        def ffn(l):
            project(segs[f"gu{l}"], norm=2 * l + 1)
            down(l)

        short_conv(0, 0)
        ffn(0)

        project(segs["q"], norm=2)
        pe.wait_ge(small_landed, 16 * 8)
        pe.wait_ge(rstd_ready, 3)
        for k in range(DC):
            for r in (xh, xl):
                for half in range(2):
                    last = mm(aux[0:NH, half, 0:TH], wf[:, k, :], r[:, k, half * TH:(half + 1) * TH].bitcast(F32),
                              start=k == 0 and r is xh, stop=k == DC - 1 and r is xl)
        last.then_inc(lf_pe, 1)

        def k_extra(m, first):
            if first:
                pe.wait_ge(lf_dve, 2)
            pe.wait_ge(head_sq, m + 1)
            if above_zero(m):
                pe.wait_ge(head_root, m)
            for half in range(2):
                last = mm(aux[:, half, 0:TH], blk[:, :], sq_chunk(m, half), start=True, stop=True)
            last.then_inc(head_sum, 1)

        def sq_chunk(m, half):
            return at1(sqb, m).rearrange("p o t -> p (o t)")[:, half * TH:(half + 1) * TH]

        def turn_v(m):
            pe.wait_ge(out_free, segs["v"].g0 + m + 1)
            if above_zero(m):
                pe.wait_ge(v_copied, m)
            for t in range(QB):
                nc.tensor.transpose(aux2[:, 0, t * P:(t + 1) * P], tt[:, t * P:(t + 1) * P], ident[:, :])
            nc.tensor.transpose(aux2[0:NS, 1, 0:P], tt[:, SEQ:T], ident[:, :]).then_inc(v_T, 1)

        def v_extra(m, first):
            pe.wait_ge(head_sq, DC + m + 1)
            pe.wait_ge(head_root, DC + m)
            for half in range(2):
                last = mm(aux[:, half, 0:TH], blk[:, :], sq_chunk(m, half), start=True, stop=True)
            last.then_inc(head_sum, 1)
            if not first:
                turn_v(m - 1)

        project(segs["k"], extra=k_extra)
        project(segs["v"], extra=v_extra)
        turn_v(DC - 1)

        pe.wait_ge(head_root, 2 * DC)
        pe.wait_ge(lf_dve, 10)
        for t in range(QB):
            nc.tensor.transpose(aux[:, 0, t * NH:(t + 1) * NH], lfT[0:NH, t * P:(t + 1) * P], ident[0:NH, 0:NH])
        nc.tensor.transpose(aux[0:NS, 0, QB * NH:(QB + 1) * NH], lfT[0:NH, SEQ:T], ident[0:NH, 0:NH]).then_inc(lf_rows, 1)
        pe.wait_ge(lf_landed, 16 * NS * NPG)
        for half in range(2):
            if half == 0:
                dst = aux[:, 1, :]
            else:
                dst = lin[0][:, 0, :]
                pe.wait_ge(out_free, segs["v"].g0 + DC)
            lf4 = lfb[:, half * 32:(half + 1) * 32, :].rearrange("p (s g) h -> p s (g h)", g=NPG)
            d4 = dst.rearrange("p (s n) -> p s n", s=4)
            mm(dst, tri[:, :], lfb[:, half * 32:(half + 1) * 32, :].rearrange("p a h -> p (a h)"), start=True, stop=False)
            for k in range(1, NPG):
                last = mm(d4[:, :, 0:(NPG - k) * NH], ones[:, :], lf4[:, :, k * NH:NPG * NH], start=False, stop=k == NPG - 1)
            last.then_inc(suffix, 1)

        pe.wait_ge(normed, 2 * DC)
        pe.wait_ge(lf_dve, 12)
        pe.wait_ge(suffix_in, 2)
        pe.wait_ge(v_copied, DC)
        items = {s: (k, i, n) for n, (s, k, i) in enumerate(B67)}
        pe.wait_ge(consts, 2)

        def item(step):
            if step not in items:
                return
            kind, i, n = items[step]
            before, uses = b67_before(n)
            if uses:
                pe.wait_ge(before, uses)
            dst = flat2(aux2)
            if kind == "qb":
                for c in range(DC):
                    last = mm(dst[:, c * P:(c + 1) * P], qT[:, c, SEQ + i:SEQ + i + 1].to_broadcast([P, P]), ident[:, :],
                              start=True, stop=True)
            elif kind == "ko":
                n_tok = P if i < QB else NS
                for c in range(DC):
                    last = nc.tensor.transpose(dst[0:n_tok, c * P:(c + 1) * P], kT[:, c, i * P:i * P + n_tok], ident[:, :])
            else:
                pe.wait_ge(zt_ready, 2 * (i + 1))
                for c in range(DC):
                    last = nc.tensor.transpose(dst[:, c * P:(c + 1) * P], ztok[:, c * P:(c + 1) * P], ident[:, :])
            last.then_inc(b67_filled, 1)

        for t in range(STEPS + 3):
            if t < STEPS:
                b, h = kv[t]
                w = (b + 1) * P
                r0 = HD * (h % 2)
                s_ps = psf["S"][t % 2]
                if above_zero(t - 1):
                    pe.wait_ge(exp_ready, t - 1)
                mm(s_ps[:, 0:w], qT[r0:r0 + HD, h // 2, b * P:(b + 1) * P], kT[r0:r0 + HD, h // 2, 0:w], start=True, stop=False)
                mm(s_ps[:, 0:w], pick[:, h:h + 1].to_broadcast([P, P]), negc[:, 0:w], start=False, stop=False)
                mm(s_ps[:, b * P:w], identr[:, :], maskr[:, :], start=False, stop=True).then_inc(s_ready, 1)
            if 1 <= t <= STEPS:
                b, h = kv[t - 1]
                pe.wait_ge(exp_ready, t)
                if above_zero(t - 2):
                    pe.wait_ge(pT_copied, t - 2)
                for j in range(b + 1):
                    last = nc.tensor.transpose(psf["PT"][(t - 1) % 2][:, j * P:(j + 1) * P],
                                               p_ring[(t - 1) % 2][:, j * P:(j + 1) * P], ident[:, :])
                last.then_inc(pT_ready, 1)
            if 2 <= t <= STEPS + 1:
                b, h = kv[t - 2]
                pe.wait_ge(pT_copied, t - 1)
                if h == 0 and b:
                    pe.wait_ge(zt_ready, 2 * b)
                for j in range(b + 1):
                    last = mm(flat2(aux)[:, h * HD:(h + 1) * HD], pt_ring[(t - 2) % 2][:, j * P:(j + 1) * P],
                              vtok[j // 2][:, j % 2, h * HD:(h + 1) * HD], start=j == 0, stop=j == b)
                last.then_inc(pv_done, 1)
            item(t)

        B2, B3 = lin[1][:, 0, :], lin[1][:, 1, :]
        pe.wait_ge(pT_copied, STEPS)
        pe.wait_ge(sm_dve, 1)
        for c in range(DC):
            last = mm(B2[0:NS, 2 * c:2 * c + 2], sm[:, 0, c * NS:(c + 1) * NS], blk[:, 0:P:HD], start=True, stop=True)
        last.then_inc(sm_pe, 1)
        pe.wait_ge(sm_dve, 3)
        mm(B2[:, P:2 * P], ones[0:NS, :], sm[0:NS, 1, :], start=True, stop=True)
        mm(B2[:, 2 * P:3 * P], ones[0:NS, :], sm[0:NS, 2, :], start=True, stop=True).then_inc(sm_pe, 1)
        pe.wait_ge(sm_dve, 7)
        nc.tensor.transpose(B3[:, 0:P], sm[:, 3, :], ident[:, :]).then_inc(sm_pe, 1)
        pe.wait_ge(sm_dve, 9)
        mm(B3[:, P:2 * P], ones[:, :], sm[:, 5, :], start=True, stop=True).then_inc(sm_pe, 1)
        pe.wait_ge(sm_dve, 14)
        mm(B3[:, 2 * P:3 * P], ones[:, :], sm[:, 5, :], start=True, stop=True).then_inc(sm_pe, 1)
        pe.wait_ge(sm_dve, 18)
        before, uses = b67_before(len(B67))
        pe.wait_ge(before, uses)
        pe.wait_ge(zt_ready, 2 * QB)
        for half in range(2):
            o = (aux, aux2)[half]
            for g in range(NPG):
                for j in range(4):
                    i = half * 4 * NPG + g * 4 + j
                    pe.wait_ge(page_landed[i % 4], 16 * ((NS * NPG + i) // 4 + 1))
                    for n in range(2):
                        last = mm(o[32 * j:32 * j + NH, n, :], sc[:, (half * 4 + j) * NPG + g, :],
                                  pages[:, i % 4, n * 512:(n + 1) * 512], start=g == 0, stop=False)
                    last.then_inc(v_used, 1)
            for j in range(4):
                for n in range(2):
                    last = mm(o[32 * j:32 * j + NH, n, :], sm[0:NS, 3, (half * 4 + j) * NH:(half * 4 + j + 1) * NH],
                              vsr[:, n * 512:(n + 1) * 512], start=False, stop=True)
            last.then_inc(v_sum, 1)
        for half in range(2):
            pe.wait_ge(osb_ready, 4 * (half + 1))
            for c in range(DC):
                last = mm(B2[:, 384 + 32 * half + 4 * c:388 + 32 * half + 4 * c], osb[:, c * P:(c + 1) * P], jsel[:, :],
                          start=True, stop=True)
            last.then_inc(o_T, 1)

        pe.wait_ge(zs_ready, 2)
        project(segs["wo"], ready=lambda k: None)
        ffn(1)

        project(segs["lg"], norm=4)
        project(segs["lx"])
        seg = segs["gates"]
        pe.wait_ge(band_landed, 16 * 4 * len(pieces))
        for m in range(LC):
            for i, band in enumerate((bandA, bandI)):
                g = seg.g0 + 2 * m + i
                pe.wait_ge(out_free, g - 1)
                cs = sources(m)
                for c in cs:
                    pe.wait_ge(conv_ready, conv0["lru"] + c + 1)
                    for half in range(2):
                        last = mm(lin[i][:, half, 0:TH], band[:, c, P * (m - c + 1):P * (m - c + 2)],
                                  xc[:, c, half * TH:(half + 1) * TH], start=c == cs[0], stop=c == cs[-1])
                last.then_inc(gate_ready, 1)
        project(segs["lo"], ready=lambda k: pe.wait_ge(z_lo, conv0["lru"] + k + 1))
        ffn(2)
        short_conv(1, 6)
        ffn(3)

        for t in range(QB + 1):
            n_tok = P if t < QB else NS
            pe.wait_ge(out_free, segs["dn3"].g0 + DC)
            if above_zero(t - 1):
                pe.wait_ge(yT_copied, t - 1)
            for c in range(DC):
                last = nc.tensor.transpose(flat2(lin[t % 2])[0:n_tok, c * P:(c + 1) * P], x[:, c, t * P:t * P + n_tok],
                                           ident[:, :])
            last.then_inc(yT_ready, 1)

    out_dmas = {"rows": 0, "k": 0}

    @block.scalar
    def _(act):
        A = nc.scalar.activation

        def split(u, p, kt):
            act.wait_ge(raw_landed[p], (u - p) * 8 + 16)
            if above_zero(u - 1):
                act.wait_ge(unit_done, u - 1)
            nc.scalar.copy(whi[:, p, 0:kt, :], wraw[:, p, 0:kt, :]).then_inc(hi_ready, 1)

        def split_next(seg, it, p, last):
            kt = seg.next_kt if last else seg.kt
            if kt:
                split(seg.u0 + 2 * it + p + 2, p, kt)

        def root(n):
            act.wait_ge(ssq_ready, n + 1)
            A(two(rstd[:, :]), pair(aux), ACT.Sqrt, bias=eps[:, 0:1], scale=1.0 / D).then_inc(root_ready, 1)

        def prep(n, m, x_new, value):
            act.wait_ge(acc_ready, 9 * n + 1 + m)
            act.wait_ge(x_new, value)
            A(at1(xh, m), at1(x, m), ACT.Copy, scale=gcol(n, m)).then_inc(xh_ready, 1)
            A(tsq[:, :], at1(x, m).rearrange("p o t -> p (o t)"), ACT.Square).then_inc(sq_ready, 1)

        def rows_move(j):
            kind, lay = STATES[j]
            widths, moves = state_rows(kind, lay)
            act.wait_ge(rows_T, j + 1)
            for i, w in enumerate(widths):
                nc.scalar.copy(rst[0:w, i, :], aux2[0:w, i, 0:P]).then_inc(rows_copied, 1)
            if kind == "lru":
                nc.scalar.copy(rst[0:9 * LC, 1, :], aux2[0:9 * LC, 1, 0:P]).then_inc(rows_copied, 1)
            act.wait_ge(rows_copied, copied[j + 1])
            for dst, part, r, n in moves:
                act.dma_start(dst, rst[r:r + n, part, :]).then_inc(rows_out, 16)
            if kind == "lru":
                act.dma_start(O["new_lru_h_prompt"][0].rearrange("b (c p) -> (b c) p", p=P), rst[0:LC, 1, :]
                              ).then_inc(rows_out, 16)
                act.dma_start(O["new_lru_h_sample"][0].rearrange("s (c p) -> (s c) p", p=P), rst[LC:9 * LC, 1, :]
                              ).then_inc(rows_out, 16)

        def seg_loop(seg, epilogue, norm=None, states=None):
            def body(it, first, last):
                for p in range(2):
                    split_next(seg, it, p, last)
                    if first and p == 0 and norm is not None:
                        root(norm)
                    epilogue(2 * it + p, seg.g0 + 2 * it + p)
                    if first and p == 1 and states is not None:
                        rows_move(states)
            loop(act, seg.halves, body)

        def conv_tap(m, g, V, w_last, b=None, off=2):
            if above_zero(V):
                act.wait_ge(conv_ready, V)
            A(ty[:, :], ext[:, off:off + T], ACT.Identity, scale=w_last, bias=0.0 if b is None else b
              ).then_inc(y_ready, 1)

        def out_proj(name, n):
            seg = segs[name]
            seg_loop(seg, lambda m, g: prep(n, m, out_free, g + 1), states=states_of.get(name))

        def short_conv(j, n):
            v0 = conv0[f"sc{j}"]
            seg_loop(segs[f"c{j}"], lambda m, g: None, norm=n)

            def h_ep(m, g):
                act.wait_ge(out_free, g + 1)
                conv_tap(m, g, v0 + m, col("sc_conv_w", j * 3 * DC + 2 * DC + m))
            seg_loop(segs[f"h{j}"], h_ep)

            def b_ep(m, g):
                act.wait_ge(out_free, g + 1)
                nc.scalar.copy(at1(hh, m), tt[:, :].unsqueeze(1)).then_inc(z_hi, 1)
            seg_loop(segs[f"b{j}"], b_ep, states=states_of[f"b{j}"])
            out_proj(f"so{j}", n + 1)

        def ffn(l):
            seg, v0 = segs[f"gu{l}"], conv0[f"ffn{l}"]

            def body(it, first, last):
                g, V = seg.g0 + 2 * it, v0 + it
                split_next(seg, it, 0, last)
                if first:
                    root(2 * l + 1)
                    if l == 1:
                        act.wait_ge(v_out, 16 * (QB // 2 + 1))
                act.wait_ge(out_free, g + 1)
                if above_zero(l * FC + it):
                    act.wait_ge(silu_ready, l * FC + it)
                conv_tap(it, g, V, col("ffn_conv_w", l * 3 * FC + 2 * FC + it), col("ffn_conv_b", l * FC + it))
                split_next(seg, it, 1, last)
                act.wait_ge(conv_ready, V + 1)
                act.wait_ge(out_free, g)
                A(tsl[:, :], ty[:, :], ACT.Silu).then_inc(silu_ready, 1)
                act.wait_ge(out_free, g + 2)
                nc.scalar.copy(at1(hh, it), tt[:, :].unsqueeze(1)).then_inc(z_hi, 1)
            loop(act, seg.halves, body)

            seg2 = segs[f"dn{l}"]
            n = 2 * l + 2

            def body2(i2, first, last):
                for a in range(2):
                    for p in range(2):
                        if not (last and a == 1):
                            split(seg2.u0 + 4 * i2 + 2 * a + p + 2, p, KH)
                        elif seg2.next_kt:
                            split(seg2.u0 + 4 * i2 + 2 * a + p + 2, p, seg2.next_kt)
                    if n < NORMS:
                        prep(n, 2 * i2 + a, out_free, seg2.g0 + 2 * i2 + a + 1)
                    if first and a == 0:
                        rows_move(states_of[f"dn{l}"])
            loop(act, DC // 2, body2)

        copied = [0]
        for kind, lay in STATES:
            copied.append(copied[-1] + len(state_rows(kind, lay)[0]) + (kind == "lru"))

        act.dma_start(x_st[:, :, :], I["x_prompt"][0].rearrange("(t p) d -> p t d", p=P)).then_inc(x_landed, 16)
        act.dma_start(xs_st[:, :], I["x_sample"].rearrange("s t d -> (s t) d")).then_inc(x_landed, 16)
        for b, r, n, src in plan:
            act.dma_start(par_st[r:r + n, b, :], src).then_inc(par_landed, 16)
        act.dma_start(pt[:, :], I["page_table"].rearrange("(o s) g -> o (s g)", o=1)).then_inc(small_landed, 16)
        act.dma_start(bf[:, :], I["fox_b_f"].rearrange("o h -> h o")).then_inc(small_landed, 16)
        for dst, src in ((qg, I["fox_q_norm"]), (kg, I["fox_k_norm"])):
            for r in (0, HD):
                act.dma_start(dst[r:r + HD, :], src.rearrange("o h -> h o")).then_inc(small_landed, 16)
        act.dma_start(wf[:, :, :], I["fox_w_f"][0].rearrange("(k p) h -> p k h", p=P)).then_inc(small_landed, 16)
        act.dma_start(O["new_sconv_sample"][:, :, 0, :], I["state_sconv"][:, :, 1, :]).then_inc(small_landed, 16)
        act.dma_start(O["new_ffn_conv_sample"][:, :, 0, :], I["state_ffn_conv"][:, :, 1, :]).then_inc(copies, 16)
        act.dma_start(O["new_lru_conv_sample"][:, :, 0:2, :], I["state_lru_conv"][:, :, 1:3, :]).then_inc(copies, 16)
        split(0, 0, 8)
        split(1, 1, 8)
        for m in range(DC):
            prep(0, m, x_in, m + 1)

        short_conv(0, 0)
        ffn(0)

        def square(m, src, value, g):
            act.wait_ge(out_free, g)
            if value:
                act.wait_ge(head_sum, m + 1)
            A(at1(sqb, m), at1(src, m), ACT.Square).then_inc(head_sq, 1)

        def head_sqrt(i):
            act.wait_ge(head_sum, i + 1)
            if above_zero(i):
                act.wait_ge(normed, i)
            A(two(ty[:, :]), pair(aux), ACT.Sqrt, bias=eps[:, 0:1], scale=1.0 / HD).then_inc(head_root, 1)

        seg_loop(segs["q"], lambda m, g: square(m, qT, 0, g + 1), norm=2)
        act.wait_ge(lf_dve, 4)
        A(tsl[0:NH, :], ty[0:NH, :], ACT.Exp, scale=-1.0).then_inc(lf_act, 1)
        act.wait_ge(lf_dve, 5)
        A(ty[0:NH, :], tsq[0:NH, :], ACT.Ln).then_inc(lf_act, 1)
        act.wait_ge(lf_dve, 11)
        A(negc[0:NH, :], tt[0:NH, 0:SEQ], ACT.Copy, scale=-1.0).then_inc(lf_act, 1)

        def k_ep(m, g):
            head_sqrt(m)
            square(m, kT, 1, g + 1)
        seg_loop(segs["k"], k_ep)

        def v_copy(m):
            act.wait_ge(v_T, m + 1)
            for i in range(2):
                nc.scalar.copy(vtok[i][:, :, ds(m * P, P)], aux2[:, 0, i * 256:(i + 1) * 256].rearrange("p (t d) -> p t d", t=2))
            nc.scalar.copy(vsr[:, ds(m * P, P)], aux2[0:NS, 1, 0:P]).then_inc(v_copied, 1)

        seg = segs["v"]

        def v_body(it, first, last):
            for p in range(2):
                m = 2 * it + p
                split_next(seg, it, p, last)
                head_sqrt(DC + m)
                if not (first and p == 0):
                    v_copy(m - 1)
        loop(act, seg.halves, v_body)
        v_copy(DC - 1)
        act.wait_ge(v_copied, DC)
        for i in range(2):
            act.dma_start(O["new_v_prompt"][0, 0, i * 256:(i + 1) * 256].rearrange("(t p) h d -> p t (h d)", p=P), vtok[i][:, :, :]
                          ).then_inc(v_out, 16)
        act.dma_start(O["new_v_sample"][0].rearrange("s t h d -> (s t) (h d)"), vsr[:, :]).then_inc(v_out, 16)
        act.wait_ge(lf_rows, 2)
        act.dma_start(O["new_logf_prompt"][0, 0].rearrange("(t p) h -> p t h", p=P), lftok[:, 0:QB, :]).then_inc(lf_out, 16)
        act.dma_start(O["new_logf_sample"][0].rearrange("s t h -> (s t) h"), lftok[0:NS, QB, :]).then_inc(lf_out, 16)

        done = {s + 1: (k, i, n) for n, (s, k, i) in enumerate(B67)}
        for t in range(STEPS + 4):
            if t < STEPS:
                b, h = kv[t]
                w = (b + 1) * P
                act.wait_ge(max_ready, t + 1)
                if above_zero(t - 1):
                    act.wait_ge(pT_ready, t - 1)
                A(p_ring[t % 2][:, 0:w], psf["S"][t % 2][:, 0:w], ACT.Exp, bias=nmax[:, t:t + 1],
                  accum_out=rsum[:, t:t + 1]).then_inc(exp_ready, 1)
            if 1 <= t <= STEPS:
                b, h = kv[t - 1]
                w = (b + 1) * P
                act.wait_ge(pT_ready, t)
                if above_zero(t - 2):
                    act.wait_ge(pv_done, t - 2)
                nc.scalar.copy(pt_ring[(t - 1) % 2][:, 0:w], psf["PT"][(t - 1) % 2][:, 0:w]).then_inc(pT_copied, 1)
            if t in done:
                kind, i, n = done[t]
                act.wait_ge(b67_filled, n + 1)
                if kind == "qb":
                    if above_zero(NPG * (i - 1)):
                        act.wait_ge(k_mult, NPG * (i - 1))
                    nc.scalar.copy(qb[:, i % 2, :], flat2(aux2)).then_inc(qb_ready, 1)
                elif kind == "ko":
                    n_tok = P if i < QB else NS
                    if above_zero(16 * i):
                        act.wait_ge(k_out, 16 * i)
                    nc.scalar.copy(kst[0:n_tok, :], flat2(aux2)[0:n_tok, :]).then_inc(b67_free, 1)
                    copied_k, uses = b67_before(n + 1)
                    act.wait_ge(copied_k, uses)
                    if i < QB:
                        dst = O["new_k_prompt"][0, 0, i * P:(i + 1) * P].rearrange("t h d -> t (h d)")
                    else:
                        dst = O["new_k_sample"][0].rearrange("s t h d -> (s t) (h d)")
                    act.dma_start(dst, kst[0:n_tok, :]).then_inc(k_out, 16)
                else:
                    nc.scalar.copy(hh[:, 0:DC, i * P:(i + 1) * P], flat2(aux2).rearrange("p (c t) -> p c t", c=DC)
                                   ).then_inc(zT_hi, 1)
        act.wait_ge(sm_dve, 12)
        A(sc[:, :, :], sc[:, :, :], ACT.Exp).then_inc(sm_act, 1)
        A(sm[:, 4, :], sm[:, 4, :], ACT.Exp).then_inc(sm_act, 1)
        for half in range(2):
            act.wait_ge(o_T, half + 1)
            nc.scalar.copy(hh[:, 0:DC, SEQ + 4 * half:SEQ + 4 * half + 4],
                           lin[1][:, 0, 384 + 32 * half:416 + 32 * half].rearrange("p (c s) -> p c s", c=DC)
                           ).then_inc(o_hi, 1)
        act.wait_ge(k_out, 16 * (QB + 1))
        out_proj("wo", 3)
        ffn(1)

        act.wait_ge(lsp_dve, 2)
        A(lsp[:, 2, :], lsp[:, 1, :], ACT.Exp, scale=-1.0).then_inc(lsp_act, 1)
        act.wait_ge(lsp_dve, 3)
        A(lsp[:, 4, :], lsp[:, 3, :], ACT.Ln).then_inc(lsp_act, 1)

        def lg_ep(m, g):
            act.wait_ge(out_free, g + 1)
            A(at1(gate, m), tt[:, :].unsqueeze(1), ACT.Gelu_apprx_tanh, bias=col("lru_b_in", m)).then_inc(gelu_ready, 1)
        seg_loop(segs["lg"], lg_ep, norm=4)
        v0 = conv0["lru"]

        def lx_ep(m, g):
            act.wait_ge(out_free, g + 1)
            act.wait_ge(conv_ready, v0 + m)
            act.wait_ge(state_kept, v0 + m)
            act.wait_ge(y_ready, v0 + m)
            if isinstance(m, int) and m == 0:
                act.wait_ge(pad_zero, 4)
            A(ext[:, 3:3 + T], tt[:, :], ACT.Identity, bias=col("lru_b_in", LC + m)).then_inc(xb_ready, 1)
            act.wait_ge(xb_ready, m + 1)
            conv_tap(m, g, v0 + m, col("lru_conv_w", 3 * LC + m), col("lru_conv_b", m), off=3)
        seg_loop(segs["lx"], lx_ep)

        act.wait_ge(conv_ready, v0 + LC)
        for hf in range(2):
            ms = range(5 * hf, 5 * hf + 5)
            for m in ms:
                act.wait_ge(gate_ready, 2 * m + 1)
                A(two(la[:, m, :]), pair(lin[0]), ACT.Sigmoid, bias=col("lru_b_a", m)).then_inc(out_free, 1)
                act.wait_ge(gate_ready, 2 * m + 2)
                A(two(lb[:, m, :]), pair(lin[1]), ACT.Sigmoid, bias=col("lru_b_i", m)).then_inc(out_free, 1)
            for m in ms:
                act.wait_ge(out_free, segs["gates"].g0 + 10 * hf + 10)
                if above_zero(m):
                    act.wait_ge(lru_q, m)
                if above_zero(5 * hf):
                    act.wait_ge(h_kept, 5 * hf)
                A(ty[:, :], la[:, m, :], ACT.Tanh, scale=lsp[:, 7, m:m + 1]).then_inc(lru_th, 1)
                act.wait_ge(lru_th, m + 1)
                A(la[:, m, :], la[:, m, :], ACT.Exp, scale=lsp[:, 7, m:m + 1]).then_inc(lru_ex, 1)
            for m in ms:
                act.wait_ge(lru_q, m + 1)
                A(xc[:, m, :], xc[:, m, :], ACT.Sqrt, scale=-1.0).then_inc(lru_root, 1)
            for m in ms:
                act.wait_ge(lru_zt, m + 1)
                nc.scalar.copy(hh[:, m, :], tz[:, :]).then_inc(z_hi, 1)
        out_proj("lo", 5)
        ffn(2)
        short_conv(1, 6)
        ffn(3)

        for t in range(QB + 1):
            n_tok = P if t < QB else NS
            act.wait_ge(yT_ready, t + 1)
            if above_zero(16 * (t // 2)):
                act.wait_ge(y_out[t % 2], 16 * (t // 2))
            nc.scalar.copy(y_st[0:n_tok, t % 2, :], flat2(lin[t % 2])[0:n_tok, :]).then_inc(yT_copied, 1)
            act.wait_ge(yT_copied, t + 1)
            dst = O["y_prompt"][0, t * P:(t + 1) * P] if t < QB else O["y_sample"].rearrange("s t d -> (s t) d")
            act.dma_start(dst, y_st[0:n_tok, t % 2, :]).then_inc(y_out[t % 2], 16)
        act.wait_ge(y_out[0], 16 * (QB // 2 + 1))
        act.wait_ge(y_out[1], 16 * (QB // 2))
        act.wait_ge(rows_out, 16 * (rows_dmas[-1] + 2))
        act.wait_ge(k_out, 16 * (QB + 1))
        act.wait_ge(v_out, 16 * (QB // 2 + 1))
        act.wait_ge(lf_out, 32)
        act.wait_ge(copies, 32)
        act.wait_ge(small_landed, 16 * 8)

    @block.vector
    def _(dve):
        V_ = nc.vector
        TT, STT, TS = V_.tensor_tensor, V_.scalar_tensor_tensor, V_.tensor_scalar

        def split(u, p, kt):
            dve.wait_ge(hi_ready, u + 1)
            TT(wlo[:, p, 0:kt, :], wraw[:, p, 0:kt, :], whi[:, p, 0:kt, :].bitcast(F32), ALU.subtract
               ).then_inc(lo_ready, 1)

        def split_next(seg, it, p, last):
            kt = seg.next_kt if last else seg.kt
            if kt:
                split(seg.u0 + 2 * it + p + 2, p, kt)

        def root(n):
            dve.wait_ge(root_ready, n + 1)
            V_.reciprocal(rstd[:, :], rstd[:, :]).then_inc(rstd_ready, 1)
            dve.wait_ge(rstd_ready, n + 1)

        def prep(n, m):
            dve.wait_ge(xh_ready, DC * n + m + 1)
            STT(out=at1(xl, m), in0=at1(x, m), scalar=gcol(n, m), in1=at1(xh, m).bitcast(F32), op0=ALU.mult, op1=ALU.subtract
                ).then_inc(xg_ready, 1)

        def seg_loop(seg, epilogue, norm=None):
            def body(it, first, last):
                for p in range(2):
                    split_next(seg, it, p, last)
                    if first and p == 0 and norm is not None:
                        root(norm)
                    dve.wait_ge(unit_done, seg.u0 + 2 * it + p + 1)
                    epilogue(2 * it + p, seg.g0 + 2 * it + p, lin[p])
            loop(dve, seg.halves, body)

        def pads(which, phase):
            extra = 2 if which > 3 else 0
            if above_zero(16 * (rows_dmas[which] + extra)):
                dve.wait_ge(rows_out, 16 * (rows_dmas[which] + extra))
            V_.memset(ext[:, 0:3], 0.0).then_inc(pad_zero, 1)
            dve.wait_ge(pad_zero, phase)

        def out_proj(name, n):
            def ep(m, g, ps):
                TT(two(at1(x, m)), pair(ps), two(at1(x, m)), ALU.add).then_inc(out_free, 1)
                prep(n, m)
            seg_loop(segs[name], ep)

        def z_split(m, V):
            dve.wait_ge(z_hi, V + 1)
            TT(at1(hl, m), tt[:, :].unsqueeze(1), at1(hh, m).bitcast(F32), ALU.subtract).then_inc(z_lo, 1)

        def short_conv(j, n, which, phase):
            v0 = conv0[f"sc{j}"]
            pads(which, phase)

            def c_ep(m, g, ps):
                TT(two(at1(cst, m)), pair(ps), two(rstd[:, :]), ALU.mult).then_inc(out_free, 1)
            seg_loop(segs[f"c{j}"], c_ep, norm=n)

            def h_ep(m, g, ps):
                V = v0 + m
                dve.wait_ge(c_scaled, j * DC + m + 1)
                if above_zero(V):
                    dve.wait_ge(y_ready, V)
                if above_zero(V):
                    dve.wait_ge(conv_ready, V)
                if above_zero(V):
                    dve.wait_ge(state_kept, V)
                TT(two(ext[:, 2:2 + T]), pair(ps), two(at1(cst, m)), ALU.mult).then_inc(out_free, 1)
                dve.wait_ge(y_ready, V + 1)
                dve.wait_ge(out_free, g + 1)
                if isinstance(m, int) and m == 0:
                    dve.wait_ge(sadd_ready, phase)
                w0 = col("sc_conv_w", j * 3 * DC + m)
                w1 = col("sc_conv_w", j * 3 * DC + DC + m)
                STT(out=ty[:, 0:SEQ], in0=ext[:, 1:1 + SEQ], scalar=w1, in1=ty[:, 0:SEQ], op0=ALU.mult, op1=ALU.add
                    ).then_inc(sc_tap, 1)
                TT(cst[:, ds(m, 1), SEQ:T], ty[:, SEQ:T].unsqueeze(1), sadd[:, ds(m, 1), :], ALU.add).then_inc(sc_tap, 1)
                dve.wait_ge(sc_tap, 2 * (j * DC + m) + 2)
                STT(out=cst[:, ds(m, 1), 0:SEQ], in0=ext[:, 0:SEQ].unsqueeze(1), scalar=w0, in1=ty[:, 0:SEQ].unsqueeze(1),
                    op0=ALU.mult, op1=ALU.add).then_inc(conv_ready, 1)
            seg_loop(segs[f"h{j}"], h_ep)

            def b_ep(m, g, ps):
                V = v0 + m
                dve.wait_ge(conv_scaled, j * DC + m + 1)
                if above_zero(V):
                    dve.wait_ge(z_lo, V)
                TT(two(tt[:, :]), pair(ps), two(at1(cst, m)), ALU.mult).then_inc(out_free, 1)
                z_split(m, V)
            seg_loop(segs[f"b{j}"], b_ep)
            out_proj(f"so{j}", n + 1)

        def ffn(l, which, phase):
            seg, v0 = segs[f"gu{l}"], conv0[f"ffn{l}"]
            pads(which, phase)

            def body(it, first, last):
                g, V = seg.g0 + 2 * it, v0 + it
                split_next(seg, it, 0, last)
                if first:
                    root(2 * l + 1)
                dve.wait_ge(unit_done, seg.u0 + 2 * it + 1)
                dve.wait_ge(y_ready, V)
                dve.wait_ge(conv_ready, V)
                dve.wait_ge(state_kept, V)
                TT(two(ext[:, 2:2 + T]), pair(lin[0]), two(rstd[:, :]), ALU.mult).then_inc(out_free, 1)
                dve.wait_ge(y_ready, V + 1)
                dve.wait_ge(out_free, g + 1)
                if first:
                    dve.wait_ge(sadd_ready, phase)
                w0 = col("ffn_conv_w", l * 3 * FC + it)
                w1 = col("ffn_conv_w", l * 3 * FC + FC + it)
                STT(out=ty[:, 0:SEQ], in0=ext[:, 1:1 + SEQ], scalar=w1, in1=ty[:, 0:SEQ], op0=ALU.mult, op1=ALU.add
                    ).then_inc(ffn_tap, 1)
                TT(ty[:, SEQ:T].unsqueeze(1), ty[:, SEQ:T].unsqueeze(1), sadd[:, ds(it, 1), :], ALU.add
                   ).then_inc(ffn_tap, 1)
                dve.wait_ge(ffn_tap, 2 * (l * FC + it) + 2)
                STT(out=ty[:, 0:SEQ], in0=ext[:, 0:SEQ], scalar=w0, in1=ty[:, 0:SEQ], op0=ALU.mult, op1=ALU.add
                    ).then_inc(conv_ready, 1)
                split_next(seg, it, 1, last)
                dve.wait_ge(unit_done, seg.u0 + 2 * it + 2)
                dve.wait_ge(scaled_ready, l * FC + it + 1)
                dve.wait_ge(z_lo, V)
                TT(two(tt[:, :]), pair(lin[1]), two(tsl[:, :]), ALU.mult).then_inc(out_free, 1)
                z_split(it, V)
            loop(dve, seg.halves, body)

            seg2 = segs[f"dn{l}"]
            n = 2 * l + 2

            def body2(i2, first, last):
                for a in range(2):
                    for p in range(2):
                        if not (last and a == 1):
                            split(seg2.u0 + 4 * i2 + 2 * a + p + 2, p, KH)
                        elif seg2.next_kt:
                            split(seg2.u0 + 4 * i2 + 2 * a + p + 2, p, seg2.next_kt)
                    m = 2 * i2 + a
                    dve.wait_ge(unit_done, seg2.u0 + 4 * i2 + 2 * a + 2)
                    TT(two(at1(x, m)), pair(lin[a]), two(at1(x, m)), ALU.add).then_inc(out_free, 1)
                    if n < NORMS:
                        prep(n, m)
            loop(dve, DC // 2, body2)

        V_.memset(eps[:, :], EPS)
        split(0, 0, 8)
        split(1, 1, 8)
        nfill = -(-NBK // 4)
        for i in range(nfill + 1 + DC):
            dve.wait_ge(filled, i + 1)
            bank = (aux, aux2)[(i % 4) // 2][:, i % 2, :]
            if i < nfill:
                n = min(512, nrows - 512 * i)
                V_.tensor_copy(par[:, 512 * i:512 * i + n], bank[:, 0:n]).then_inc(fill_free, 1)
            elif i == nfill:
                V_.tensor_copy(x[:, :, SEQ:T], bank[:, 0:DC * NS].rearrange("p (c s) -> p c s", c=DC)).then_inc(fill_free, 1)
                dve.wait_ge(fill_free, i + 1)
            else:
                V_.tensor_copy(x[:, i - nfill - 1, 0:SEQ], bank).then_inc(x_in, 1)
        for m in range(DC):
            dve.wait_ge(x_in, m + 1)
            prep(0, m)

        short_conv(0, 0, 0, 1)
        ffn(0, 1, 2)

        def q_ep(m, g, ps):
            TT(two(at1(qT, m)), pair(ps), two(rstd[:, :]), ALU.mult).then_inc(out_free, 1)
        seg_loop(segs["q"], q_ep, norm=2)

        n = [0]

        def lf(ins):
            n[0] += 1
            ins.then_inc(lf_dve, 1)
            dve.wait_ge(lf_dve, n[0])
        dve.wait_ge(rows_out, 16 * rows_dmas[2])
        lf(V_.memset(negc[:, :].bitcast(F32), 0.0))
        dve.wait_ge(lf_pe, 1)
        lf(TT(two(tt[0:NH, :]), pair(aux)[0:NH], two(rstd[0:NH, :]), ALU.mult))
        lf(TS(tt[0:NH, :], tt[0:NH, :], bf[:, 0:1], None, ALU.add))
        lf(STT(out=ty[0:NH, :], in0=tt[0:NH, :], scalar=-1.0, in1=tt[0:NH, :], op0=ALU.mult, op1=ALU.max))
        dve.wait_ge(lf_act, 1)
        lf(TS(tsq[0:NH, :], tsl[0:NH, :], 1.0, None, ALU.add))
        lf(STT(out=tsl[0:NH, :], in0=tsq[0:NH, :], scalar=1.0, in1=tsl[0:NH, :], op0=ALU.subtract, op1=ALU.subtract))
        dve.wait_ge(lf_act, 2)
        lf(V_.reciprocal(tsq[0:NH, :], tsq[0:NH, :]))
        lf(TT(tsl[0:NH, :], tsl[0:NH, :], tsq[0:NH, :], ALU.mult))
        lf(TT(ty[0:NH, :], ty[0:NH, :], tsl[0:NH, :], ALU.subtract))
        lf(STT(out=lfT[:, :], in0=tt[0:NH, :], scalar=0.0, in1=ty[0:NH, :], op0=ALU.min, op1=ALU.subtract))
        lf(V_.tensor_tensor_scan(tt[0:NH, 0:SEQ], ones[0:NH, 0:1].to_broadcast([NH, SEQ]), lfT[:, 0:SEQ], 0.0,
                                 ALU.mult, ALU.add))
        dve.wait_ge(lf_act, 3)
        lf(STT(out=negc[32:32 + NH, :], in0=tt[0:NH, 0:SEQ], scalar=-1.0, in1=negc[0:NH, :].bitcast(F32),
               op0=ALU.mult, op1=ALU.subtract))

        def normalise(i, tile, m, gain):
            dve.wait_ge(head_root, i + 1)
            V_.reciprocal(ty[:, :], ty[:, :]).then_inc(head_recip, 1)
            dve.wait_ge(head_recip, i + 1)
            STT(out=at1(tile, m), in0=at1(tile, m), scalar=gain[:, 0:1], in1=ty[:, :].unsqueeze(1),
                op0=ALU.mult, op1=ALU.mult).then_inc(normed, 1)

        dve.wait_ge(small_landed, 16 * 8)
        V_.tensor_scalar(qg[:, :], qg[:, :], HD ** -0.5, None, ALU.mult).then_inc(lf_dve, 1)
        dve.wait_ge(lf_dve, 13)

        def k_ep(m, g, ps):
            TT(two(at1(kT, m)), pair(ps), two(rstd[:, :]), ALU.mult).then_inc(out_free, 1)
            normalise(m, qT, m, qg)
        seg_loop(segs["k"], k_ep)

        def v_ep(m, g, ps):
            if above_zero(m):
                dve.wait_ge(v_T, m)
            TT(two(tt[:, :]), pair(ps), two(rstd[:, :]), ALU.mult).then_inc(out_free, 1)
            normalise(DC + m, kT, m, kg)
        seg_loop(segs["v"], v_ep)

        dve.wait_ge(v_T, DC)
        dve.wait_ge(lf_rows, 1)
        V_.tensor_copy(lftok[:, 0:QB, :], aux[:, 0, 0:QB * NH].rearrange("p (t h) -> p t h", h=NH))
        V_.tensor_copy(lftok[0:NS, QB, :], aux[0:NS, 0, QB * NH:(QB + 1) * NH]).then_inc(lf_rows, 1)
        for half in range(2):
            dve.wait_ge(suffix, half + 1)
            if half == 0:
                dve.wait_ge(suffix, 2)
            V_.tensor_copy(lfb[:, 32 * half:32 * half + 32, :].rearrange("p a h -> p (a h)"),
                           aux[:, 1, :] if half == 0 else lin[0][:, 0, :]).then_inc(suffix_in, 1)

        items = {s + 1: (k, i, m) for m, (s, k, i) in enumerate(B67)}
        for t in range(STEPS + 5):
            if t < STEPS:
                b, h = kv[t]
                w = (b + 1) * P
                dve.wait_ge(s_ready, t + 1)
                V_.reduce_max(nmax[:, t:t + 1], psf["S"][t % 2][:, 0:w], AX.X, negate=True).then_inc(max_ready, 1)
            g = t - 2
            if 0 <= g < NS * NPG:
                dve.wait_ge(k_mult, g + 1)
                V_.reduce_sum(sc[:, g, :], pages[:, g % 4, :].rearrange("p (h d) -> p h d", d=HD), AX.X
                              ).then_inc(k_reduced, 1)
            if t % NH == 2 and t > NH:
                b = (t - 2) // NH - 1
                dve.wait_ge(pv_done, NH * (b + 1))
                if above_zero(b):
                    dve.wait_ge(zT_hi, b)
                V_.reciprocal(rinv[:, :], rsum[:, NH * b:NH * (b + 1)]).then_inc(zt_step, 1)
                dve.wait_ge(zt_step, b + 1)
                for half in range(2):
                    hs = NH // 2
                    TT(ztok[:, half * 512:(half + 1) * 512].rearrange("p (h d) -> p h d", d=HD),
                       aux[:, half, :].rearrange("p (h d) -> p h d", d=HD),
                       rinv[:, half * hs:(half + 1) * hs].unsqueeze(2).to_broadcast([P, hs, HD]), ALU.mult
                       ).then_inc(zt_ready, 1)
            if t in items and items[t][0] == "zT":
                i = items[t][1]
                dve.wait_ge(zT_hi, i + 1)
                TT(hl[:, 0:DC, i * P:(i + 1) * P], flat2(aux2).rearrange("p (c t) -> p c t", c=DC),
                   hh[:, 0:DC, i * P:(i + 1) * P].bitcast(F32), ALU.subtract).then_inc(b67_free, 1)

        n[0] = 0

        def smx(ins):
            n[0] += 1
            ins.then_inc(sm_dve, 1)
            dve.wait_ge(sm_dve, n[0])
        B2, B3 = lin[1][:, 0, :], lin[1][:, 1, :]
        spread = ident[0:NS, 0:NS].unsqueeze(2).to_broadcast([NS, NS, NH])

        def sh(i, n_=P):
            return sm[0:n_, i, :].rearrange("p (s h) -> p s h", h=NH)

        sc4 = sc[:, :, :].rearrange("p (s g) h -> p s g h", g=NPG)

        def over_pages(ap):
            return ap.rearrange("p (s h) -> p s h", h=NH).unsqueeze(2).to_broadcast([P, NS, NPG, NH])
        dve.wait_ge(pv_done, STEPS)
        smx(TT(sm[:, 0, 0:DC * NS].rearrange("p (c s) -> p c s", c=DC), qT[:, :, SEQ:T], kT[:, :, SEQ:T], ALU.mult))
        dve.wait_ge(sm_pe, 1)
        smx(TT(sh(1, NS), B2[0:NS, 0:NH].unsqueeze(1).to_broadcast([NS, NS, NH]), spread, ALU.mult))
        smx(TT(sh(2, NS), lftok[0:NS, QB, :].unsqueeze(1).to_broadcast([NS, NS, NH]), spread, ALU.mult))
        dve.wait_ge(sm_pe, 2)
        smx(TT(sc[:, :, :], sc[:, :, :], lfb[:, :, :], ALU.add))
        for s in range(NS):
            ins = TT(sc4[:, s], sc4[:, s], B2[:, 2 * P + s * NH:2 * P + (s + 1) * NH].unsqueeze(1).to_broadcast([P, NPG, NH]),
                     ALU.add)
        smx(ins)
        smx(V_.tensor_reduce(sh(3), sc[:, :, :].rearrange("p (s g) h -> p s h g", g=NPG), AX.X, ALU.max))
        smx(TT(sm[:, 3, :], sm[:, 3, :], B2[:, P:2 * P], ALU.max))
        dve.wait_ge(sm_pe, 3)
        smx(V_.reduce_max(smal[:, 0, 0:1], B3[:, 0:P], AX.X))
        smx(TS(sm[:, 5, :], ident[:, :], smal[:, 0, 0:1], None, ALU.mult))
        smx(V_.tensor_copy(sm[:, 4, :], B2[:, P:2 * P]))
        dve.wait_ge(sm_pe, 4)
        smx(TT(sm[:, 4, :], sm[:, 4, :], B3[:, P:2 * P], ALU.subtract))
        for s in range(NS):
            ins = TT(sc4[:, s], sc4[:, s], B3[:, P + s * NH:P + (s + 1) * NH].unsqueeze(1).to_broadcast([P, NPG, NH]),
                     ALU.subtract)
        smx(ins)
        dve.wait_ge(sm_act, 2)
        smx(V_.tensor_reduce(sh(5), sc[:, :, :].rearrange("p (s g) h -> p s h g", g=NPG), AX.X, ALU.add))
        smx(STT(out=sm[:, 5, :], in0=sm[:, 4, :], scalar=1.0 / P, in1=sm[:, 5, :], op0=ALU.mult, op1=ALU.add))
        dve.wait_ge(sm_pe, 5)
        smx(V_.reciprocal(sm[:, 0, :], B3[:, 2 * P:3 * P]))
        for s in range(NS):
            ins = TT(sc4[:, s], sc4[:, s], sm[:, 0, s * NH:(s + 1) * NH].unsqueeze(1).to_broadcast([P, NPG, NH]), ALU.mult)
        smx(ins)
        smx(TT(sm[:, 4, :], sm[:, 4, :], sm[:, 0, :], ALU.mult))
        smx(TT(sh(3, NS), sh(4, NS), spread, ALU.mult))
        for half in range(2):
            dve.wait_ge(v_sum, half + 1)
            if above_zero(half):
                dve.wait_ge(o_T, half)
            dve.wait_ge(osb_zero, 1)
            for j in range(4):
                r = 32 * j
                TT(osb[r:r + NH, :].rearrange("p (h d) -> p h d", d=HD),
                   flat2((aux, aux2)[half])[r:r + NH, :].rearrange("p (h d) -> p h d", d=HD),
                   ident[r:r + NH, r:r + NH].unsqueeze(2).to_broadcast([NH, NH, HD]), ALU.mult).then_inc(osb_ready, 1)
            dve.wait_ge(o_hi, half + 1)
            TT(hl[:, 0:DC, SEQ + 4 * half:SEQ + 4 * half + 4],
               B2[:, 384 + 32 * half:416 + 32 * half].rearrange("p (c s) -> p c s", c=DC),
               hh[:, 0:DC, SEQ + 4 * half:SEQ + 4 * half + 4].bitcast(F32), ALU.subtract).then_inc(zs_ready, 1)
        out_proj("wo", 3)
        ffn(1, 2, 3)

        n[0] = 0

        def ls(ins):
            n[0] += 1
            ins.then_inc(lsp_dve, 1)
            dve.wait_ge(lsp_dve, n[0])
        lam = par[:, rows["lru_lambda"]:rows["lru_lambda"] + LC]
        ls(TS(lsp[:, 0, :], lam, -1.0, 0.0, ALU.mult, ALU.max))
        ls(STT(out=lsp[:, 1, :], in0=lam, scalar=-1.0, in1=lam, op0=ALU.mult, op1=ALU.max))
        dve.wait_ge(lsp_act, 1)
        ls(TS(lsp[:, 3, :], lsp[:, 2, :], 1.0, None, ALU.add))
        ls(STT(out=lsp[:, 5, :], in0=lsp[:, 3, :], scalar=1.0, in1=lsp[:, 2, :], op0=ALU.subtract, op1=ALU.subtract))
        ls(V_.reciprocal(lsp[:, 6, :], lsp[:, 3, :]))
        ls(TT(lsp[:, 5, :], lsp[:, 5, :], lsp[:, 6, :], ALU.mult))
        dve.wait_ge(lsp_act, 2)
        ls(TT(lsp[:, 5, :], lsp[:, 4, :], lsp[:, 5, :], ALU.subtract))
        ls(TT(lsp[:, 7, :], lsp[:, 5, :], lsp[:, 0, :], ALU.add))
        ls(TS(lsp[:, 7, :], lsp[:, 7, :], -LRU_C, None, ALU.mult))
        pads(3, 4)

        def lg_ep(m, g, ps):
            if above_zero(m):
                dve.wait_ge(gelu_ready, m)
            TT(two(tt[:, :]), pair(ps), two(rstd[:, :]), ALU.mult).then_inc(out_free, 1)
        seg_loop(segs["lg"], lg_ep, norm=4)
        v0 = conv0["lru"]

        def lx_ep(m, g, ps):
            V = v0 + m
            if isinstance(m, int) and m == 0:
                dve.wait_ge(gelu_ready, LC)
                dve.wait_ge(sadd_ready, 4)
            if above_zero(m):
                dve.wait_ge(xb_ready, m)
            TT(two(tt[:, :]), pair(ps), two(rstd[:, :]), ALU.mult).then_inc(out_free, 1)
            dve.wait_ge(y_ready, V + 1)
            w0, w1, w2 = (col("lru_conv_w", k * LC + m) for k in range(3))
            STT(out=ty[:, 0:SEQ], in0=ext[:, 2:2 + SEQ], scalar=w2, in1=ty[:, 0:SEQ], op0=ALU.mult, op1=ALU.add
                ).then_inc(lru_tap, 1)
            TT(xc[:, ds(m, 1), SEQ:T], ty[:, SEQ:T].unsqueeze(1), sadd[:, ds(m, 1), :], ALU.add).then_inc(lru_tap, 1)
            dve.wait_ge(lru_tap, 3 * m + 2)
            STT(out=ty[:, 0:SEQ], in0=ext[:, 1:1 + SEQ], scalar=w1, in1=ty[:, 0:SEQ], op0=ALU.mult, op1=ALU.add
                ).then_inc(lru_tap, 1)
            dve.wait_ge(lru_tap, 3 * m + 3)
            STT(out=xc[:, ds(m, 1), 0:SEQ], in0=ext[:, 0:SEQ].unsqueeze(1), scalar=w0, in1=ty[:, 0:SEQ].unsqueeze(1),
                op0=ALU.mult, op1=ALU.add).then_inc(conv_ready, 1)
        seg_loop(segs["lx"], lx_ep)

        for hf in range(2):
            ms = range(5 * hf, 5 * hf + 5)
            for m in ms:
                dve.wait_ge(lru_ex, m + 1)
                dve.wait_ge(lru_ix, m + 1)
                if above_zero(m):
                    dve.wait_ge(lru_q, m)
                TT(tsl[:, :], la[:, m, :], la[:, m, :], ALU.mult).then_inc(lru_b, 1)
                dve.wait_ge(lru_b, 4 * hf * 5 + (m - 5 * hf) + 1)
                STT(out=xc[:, m, :], in0=tsl[:, :], scalar=1.0, in1=ty[:, :], op0=ALU.add, op1=ALU.mult
                    ).then_inc(lru_q, 1)
            for m in ms:
                base = 20 * hf + 5 + 3 * (m - 5 * hf)
                dve.wait_ge(lru_root, m + 1)
                if above_zero(m):
                    dve.wait_ge(lru_h, m)
                TT(tt[:, :], lb[:, m, :], xc[:, m, :], ALU.mult).then_inc(lru_b, 1)
                h0 = rows["state_lru_h"]
                TT(stmp[:, 0, :], la[:, m, SEQ:T], par[:, h0 + m:h0 + m + (NS - 1) * LC + 1:LC], ALU.mult
                   ).then_inc(lru_b, 1)
                dve.wait_ge(lru_b, base + 2)
                if above_zero(m):
                    dve.wait_ge(h_kept, m)
                if above_zero(m):
                    dve.wait_ge(lru_zt, m)
                TT(ty[:, SEQ:T], tt[:, SEQ:T], stmp[:, 0, :], ALU.add).then_inc(lru_b, 1)
                dve.wait_ge(lru_b, base + 3)
                V_.tensor_tensor_scan(ty[:, 0:SEQ], la[:, m, 0:SEQ], tt[:, 0:SEQ], 0.0, ALU.mult, ALU.add
                                      ).then_inc(lru_h, 1)
                dve.wait_ge(lru_h, m + 1)
                dve.wait_ge(z_lo, v0 + m)
                TT(tz[:, :], ty[:, :], gate[:, m, :], ALU.mult).then_inc(lru_zt, 1)
                dve.wait_ge(z_hi, v0 + m + 1)
                TT(hl[:, m, :], tz[:, :], hh[:, m, :].bitcast(F32), ALU.subtract).then_inc(z_lo, 1)
        out_proj("lo", 5)
        ffn(2, 4, 5)
        short_conv(1, 6, 5, 6)
        ffn(3, 6, 7)

    @block.gpsimd
    def _(pool):
        G = nc.gpsimd
        TT = G.tensor_tensor

        steps = [0]

        def link(ins):
            steps[0] += 1
            ins.then_inc(sadd_step, 1)
            pool.wait_ge(sadd_step, steps[0])
        for tile in (ones, ident, blk, jsel):
            link(G.memset(tile[:, :], 1.0 if tile is ones else 0.0))
        link(G.memset(tz[:, 0:P], 0.0))
        link(G.memset(tz[:, P:P + NH], 0.0))
        link(G.affine_select(out=tri[:, :], in_=ones[:, :], compare_op=ALU.is_gt, fill=0.0, base=0, pattern=[[-1, P]],
                             channel_multiplier=1))
        link(G.memset(blk[0:HD, 0:HD], 1.0))
        link(G.memset(blk[HD:P, HD:P], 1.0))
        for j in range(4):
            link(G.memset(jsel[32 * j:32 * j + 32, j:j + 1], 1.0))
        link(G.affine_select(out=tz[:, 0:P], in_=tz[:, 0:P], compare_op=ALU.is_ge, fill=MASK_VALUE, base=0, pattern=[[-1, P]],
                             channel_multiplier=1))
        for base in (0, -32):
            link(G.affine_select(out=tz[:, P:P + NH], in_=tz[:, P:P + NH], compare_op=ALU.not_equal, fill=1.0, base=base,
                                 pattern=[[-1, NH]], channel_multiplier=1))
        link(G.affine_select(out=ident[:, :], in_=ident[:, :], compare_op=ALU.not_equal, fill=1.0, base=0, pattern=[[-1, P]],
                             channel_multiplier=1))
        G.memset(acc[:, :], 0.0).then_inc(acc_ready, 1)
        G.tensor_copy(identr[:, :], ident[:, :]).then_inc(consts, 1)
        G.tensor_copy(maskr[:, :], tz[:, 0:P])
        G.tensor_copy(pick[:, :], tz[:, P:P + NH]).then_inc(consts, 1)

        def prep(n, m):
            pool.wait_ge(sq_ready, DC * n + m + 1)
            pool.wait_ge(acc_ready, 9 * n + 1 + m)
            TT(acc[:, :], acc[:, :], tsq[:, :], ALU.add).then_inc(acc_ready, 1)

        def reset(n):
            pool.wait_ge(ssq_ready, n + 1)
            G.memset(acc[:, :], 0.0).then_inc(acc_ready, 1)
            pool.wait_ge(rstd_ready, n + 1)

        def sample_add(weights, state, chunks, taps, lay, s_stride, phase):
            r0, w0 = rows[state] + lay * NS * s_stride, rows[weights] + lay * (taps + 1) * chunks
            old = par[:, r0:r0 + NS * s_stride].rearrange("p (s k c) -> p k c s", s=NS, k=taps)
            if above_zero(phase - 1):
                pool.wait_ge(sadd_ready, phase - 1)
            for k in range(taps):
                w = par[:, w0 + k * chunks:w0 + (k + 1) * chunks].unsqueeze(2).to_broadcast([P, chunks, NS])
                dst = sadd if k == 0 else stmp
                link(TT(dst[:, 0:chunks, :], old[:, k], w, ALU.mult))
                if k == taps - 1:
                    TT(sadd[:, 0:chunks, :], sadd[:, 0:chunks, :], stmp[:, 0:chunks, :], ALU.add).then_inc(sadd_ready, 1)
                elif k:
                    link(TT(sadd[:, 0:chunks, :], sadd[:, 0:chunks, :], stmp[:, 0:chunks, :], ALU.add))

        def chunk_sum(n):
            with pool.Fori(0, DC) as m:
                prep(n, m)

        def keep(m, q, chunks):
            G.tensor_copy(sto[:, 0:q * chunks].rearrange("p (q c) -> p q c", c=chunks)[:, :, ds(m, 1)],
                          ext[:, SEQ:SEQ + q].unsqueeze(2)).then_inc(state_kept, 1)

        def short_conv(j, n, which, phase):
            v0 = conv0[f"sc{j}"]
            if above_zero(which):
                pool.wait_ge(rows_T, which)
            sample_add("sc_conv_w", "state_sconv", DC, 2, j, 2 * DC, phase)
            reset(n)
            with pool.Fori(0, DC) as m:
                pool.wait_ge(out_free, segs[f"c{j}"].g0 + m + 1)
                TT(at1(cst, m), at1(cst, m), rstd[:, :].unsqueeze(1), ALU.mult).then_inc(c_scaled, 1)
            with pool.Fori(0, DC) as m:
                pool.wait_ge(out_free, segs[f"h{j}"].g0 + m + 1)
                keep(m, 10, DC)
                pool.wait_ge(conv_ready, v0 + m + 1)
                TT(at1(cst, m), at1(cst, m), rstd[:, :].unsqueeze(1), ALU.mult).then_inc(conv_scaled, 1)
            chunk_sum(n + 1)

        def ffn(l, which, phase):
            seg, v0 = segs[f"gu{l}"], conv0[f"ffn{l}"]
            pool.wait_ge(rows_T, which)
            sample_add("ffn_conv_w", "state_ffn_conv", FC, 2, l, 2 * FC, phase)
            reset(2 * l + 1)
            with pool.Fori(0, FC) as it:
                pool.wait_ge(out_free, seg.g0 + 2 * it + 1)
                keep(it, 10, FC)
                pool.wait_ge(silu_ready, l * FC + it + 1)
                TT(tsl[:, :], tsl[:, :], rstd[:, :], ALU.mult).then_inc(scaled_ready, 1)
            if 2 * l + 2 < NORMS:
                chunk_sum(2 * l + 2)

        pool.wait_ge(fill_free, -(-NBK // 4))
        chunk_sum(0)
        short_conv(0, 0, 0, 1)
        ffn(0, 1, 2)

        reset(2)
        pool.wait_ge(unit_done, segs["dn0"].u0 + 16)
        pool.wait_ge(small_landed, 16 * 8)
        with pool.Fori(0, NS * NPG) as i:
            idx = pool.value_load(pt[0:1, ds(i, 1)], min_val=0, max_val=NPOOL - 1)
            pool.dma_start(lfb[:, ds(i, 1), :], I["cache_logf"][0][ds(idx, 1)].rearrange("a p h -> p a h")
                           ).then_inc(lf_landed, 16)
        with pool.Fori(0, NS // 2) as i:
            for s in range(2):
                for g in range(NPG):
                    n = s * NPG + g
                    if g == 0:
                        pool.wait_ge(qb_ready, 2 * i + s + 1)
                    pool.wait_ge(page_landed[n % 4], 64 * i + 16 * (n // 4 + 1))
                    TT(pages[:, n % 4, :], pages[:, n % 4, :], qb[:, s, :], ALU.mult).then_inc(k_mult, 1)
        pool.wait_ge(pT_ready, STEPS)
        G.memset(osb[:, :], 0.0).then_inc(osb_zero, 1)
        chunk_sum(3)
        ffn(1, 2, 3)

        v0 = conv0["lru"]
        pool.wait_ge(rows_T, 3)
        sample_add("lru_conv_w", "state_lru_conv", LC, 3, 0, 3 * LC, 4)
        reset(4)
        with pool.Fori(0, LC) as m:
            pool.wait_ge(xb_ready, m + 1)
            keep(m, 11, LC)
        pool.wait_ge(unit_done, segs["lx"].u0 + LC)
        G.memset(bandA[:, :, :], 0.0).then_inc(band_zero, 1)
        G.memset(bandI[:, :, :], 0.0).then_inc(band_zero, 1)
        for hf in range(2):
            for m in range(5 * hf, 5 * hf + 5):
                pool.wait_ge(out_free, segs["gates"].g0 + 2 * m + 2)
                TT(lb[:, m, :], lb[:, m, :], xc[:, m, :], ALU.mult).then_inc(lru_ix, 1)
            for m in range(5 * hf, 5 * hf + 5):
                pool.wait_ge(lru_h, m + 1)
                G.tensor_copy(hst[:, :, m], ty[:, SEQ - 1:T]).then_inc(h_kept, 1)
        chunk_sum(5)
        ffn(2, 4, 5)
        short_conv(1, 6, 5, 6)
        ffn(3, 6, 7)

    psum.close()


def _outs(i):
    B, SEQ, D = i["x_prompt"].shape
    S_ = i["x_sample"].shape[0]
    NA, _, r, _ = i["state_sconv"].shape
    NB, _, _, H, HDIM = i["cache_k"].shape
    NC, _, LW = i["state_lru_h"].shape
    rl = i["state_lru_conv"].shape[2]
    DEPTH, _, rf, F = i["state_ffn_conv"].shape
    return [("y_prompt", (B, SEQ, D)), ("y_sample", (S_, 1, D)),
            ("new_sconv_prompt", (NA, B, r, D)), ("new_sconv_sample", (NA, S_, r, D)),
            ("new_k_prompt", (NB, B, SEQ, H, HDIM)), ("new_v_prompt", (NB, B, SEQ, H, HDIM)), ("new_logf_prompt", (NB, B, SEQ, H)),
            ("new_k_sample", (NB, S_, 1, H, HDIM)), ("new_v_sample", (NB, S_, 1, H, HDIM)), ("new_logf_sample", (NB, S_, 1, H)),
            ("new_lru_h_prompt", (NC, B, LW)), ("new_lru_h_sample", (NC, S_, LW)),
            ("new_lru_conv_prompt", (NC, B, rl, LW)), ("new_lru_conv_sample", (NC, S_, rl, LW)),
            ("new_ffn_conv_prompt", (DEPTH, B, rf, F)), ("new_ffn_conv_sample", (DEPTH, S_, rf, F))]


def kernel(**inputs):
    import numpy as np
    import concourse.bacc as bacc
    from concourse.bass_utils import run_bass_kernel_spmd

    nc = bacc.Bacc("TRN2", target_bir_lowering=False, num_devices=1)
    arrays = {name: np.ascontiguousarray(a) for name, a in inputs.items()}
    ins = {name: nc.dram_tensor(name, a.shape, mybir.dt.from_np(a.dtype), kind="ExternalInput").ap()
           for name, a in arrays.items()}
    outs = {name: nc.dram_tensor(name, shape, F32, kind="ExternalOutput").ap() for name, shape in _outs(arrays)}
    hybrid_step(nc, ins, outs)
    result = run_bass_kernel_spmd(nc, [arrays], core_ids=[0]).results[0]
    return tuple(result[name] for name, _ in _outs(arrays))
```

```python
from contextlib import ExitStack

import concourse.bass as bass
from concourse import mybir

P = 128
F32 = mybir.dt.float32
F32R = mybir.dt.float32r
I32 = mybir.dt.int32
ALU = mybir.AluOpType
ACT = mybir.ActivationFunctionType
AX = mybir.AxisListType
ds = bass.ds

EPS = 1e-6
LRU_C = 8.0
MASK_VALUE = -1e30
NS = 8
HD = 64


def hybrid_step(nc, I, O):
    D = I["x_prompt"].shape[2]
    SEQ = I["x_prompt"].shape[1]
    T = SEQ + NS
    TH = T // 2
    DC = D // P
    FF = I["ffn_w_gate"].shape[2]
    FC = FF // P
    TILES = 13
    KH = FC // 2
    LW = I["lru_w_out"].shape[1]
    LC = LW // P
    LB = I["lru_w_a"].shape[2]
    NH = D // HD
    NPG = I["page_table"].shape[1]
    NPOOL = I["cache_k"].shape[1]
    DEPTH = I["mix_norm"].shape[0]
    QB = SEQ // P
    assert T % 4 == 0 and P * 5 == LB * 8 and LC == 10 and FC % 2 == 0 and DC == 8 and NH == 16

    class Seg:
        pass

    LGA = 4
    segs, order = {}, []
    nu = ng = 0
    for name, units, kt, upg in (
            [("c0", 8, 8, 1), ("h0", 8, 8, 1), ("b0", 8, 8, 1), ("so0", 8, 8, 1), ("gu0", 2 * FC, 8, 1), ("dn0", 16, KH, 2),
             ("q", 8, 8, 1), ("k", 8, 8, 1), ("v", 8, 8, 1), ("wo", 8, 8, 1), ("gu1", 2 * FC, 8, 1), ("dn1", 16, KH, 2),
             ("lx", LC, 8, 1), ("gates0", 0, 0, 1), ("lgA", LGA, 8, 1), ("gates1", 0, 0, 1), ("lgB", LC - LGA, 8, 1),
             ("lo", 8, LC, 1), ("gu2", 2 * FC, 8, 1), ("dn2", 16, KH, 2),
             ("c1", 8, 8, 1), ("h1", 8, 8, 1), ("b1", 8, 8, 1), ("so1", 8, 8, 1), ("gu3", 2 * FC, 8, 1), ("dn3", 16, KH, 2)]):
        s = Seg()
        s.name, s.units, s.kt, s.u0, s.g0 = name, units, kt, nu, ng
        nu += units
        ng += units // upg if units else LC
        s.halves = units // 2
        segs[name] = s
        if units:
            order.append(s)
    for a, b in zip(order, order[1:] + [None]):
        a.next_kt = b.kt if b and b.name != "wo" else None

    def gsrc(name):
        j = int(name[-1]) if name[-1].isdigit() else 0
        W = {"c": (I["sc_w_in"], D), "h": (I["sc_w_in"], 2 * D), "b": (I["sc_w_in"], 0), "so": (I["sc_w_out"], 0),
             "q": (I["fox_w_qkv"], 0), "k": (I["fox_w_qkv"], D), "v": (I["fox_w_qkv"], 2 * D), "wo": (I["fox_w_o"], 0),
             "lgA": (I["lru_w_in"], 0), "lgB": (I["lru_w_in"], LGA * P), "lx": (I["lru_w_in"], LW),
             "lo": (I["lru_w_out"], 0), "dn": (I["ffn_w_down"], 0)}
        w, c = W[name.rstrip("0123")]
        return w[j].rearrange("(k p) n -> p k n", p=P), c

    rows = {}
    nrows = 0
    plan = []
    for name in ("mix_norm", "ffn_norm", "sc_conv_w", "state_sconv", "ffn_conv_w", "ffn_conv_b", "state_ffn_conv",
                 "lru_b_in", "lru_conv_w", "lru_conv_b", "lru_b_a", "lru_b_i", "lru_lambda", "state_lru_h",
                 "state_lru_conv"):
        ap = I[name]
        n = 1
        for d in ap.shape:
            n *= d
        n //= P
        rows[name] = nrows
        dims = " ".join(f"d{i}" for i in range(len(ap.shape)))
        flat = ap.rearrange(f"{dims} -> ({dims})").rearrange("(r p) -> r p", p=P)
        at = 0
        while at < n:
            b, r = (nrows + at) // P, (nrows + at) % P
            full = 0 if r else (n - at) // P
            take = full * P or min(n - at, P - r)
            src = flat[at:at + take, :]
            plan.append((b, max(full, 1), r, P if full else take,
                         src.rearrange("(b r) p -> r b p", r=P) if full else src.unsqueeze(1)))
            at += take
        nrows += n
    NBK = -(-nrows // P)

    at = [16512]

    def place(name, shape, dt, offset=None):
        size = 4
        for d in shape[1:]:
            size *= d
        if offset is None:
            offset = at[0]
            at[0] += -(-size // 32) * 32
        return nc.alloc_sbuf_tensor_at(name, shape, dt, offset=offset)

    SLOT = 4 * T
    x = place("x", [P, DC, T], F32)
    XG = at[0]
    xh = place("xh", [P, DC, T], F32R)
    xl = place("xl", [P, DC, T], F32R)
    wraw = place("wraw", [P, 2, KH, P], F32)
    whi = place("whi", [P, 2, KH, P], F32R)
    wlo = place("wlo", [P, 2, KH, P], F32R)
    WORK = at[0]
    hh = place("hh", [P, FC, T], F32R)
    hl = place("hl", [P, FC, T], F32R)
    par = place("par", [P, nrows], F32)
    TMP = at[0]
    ext = place("ext", [P, T + 4], F32)
    rstd = place("rstd", [P, T], F32)
    acc = place("acc", [P, T], F32)
    tt = place("tt", [P, T], F32)
    ty = place("ty", [P, T], F32)
    tsl = place("tsl", [P, T], F32)
    tsq = place("tsq", [P, T], F32)
    tz = place("tz", [P, T], F32)
    ident = place("ident", [P, P], F32)
    ones = place("ones", [P, P], F32)
    blk = place("blk", [P, P], F32)
    sto_at = at[0]
    sto = place("sto", [P, 11 * FC], F32)
    sadd = place("sadd", [P, FC, NS], F32)
    stmp = place("stmp", [P, FC, NS], F32)
    eps = place("eps", [P, 1], F32)
    pt_at = at[0]
    pt = place("pt", [1, NS * NPG], I32)
    bf = place("bf", [NH, 1], F32)
    qg = place("qg", [P, 1], F32)
    kg = place("kg", [P, 1], F32)
    jsel = place("jsel", [P, 4], F32)
    vsr = place("vsr", [NS, D], F32)
    identr = place("identr", [P, P], F32R)
    maskr = place("maskr", [P, P], F32R)
    pick = place("pick", [P, NH], F32R)
    head_mask = place("head_mask", [P, NH], F32)
    pickm = place("pickm", [P, NH], F32R)
    wf = place("wf", [P, DC, NH], F32)
    tri = place("tri", [P, P], F32)
    assert at[0] <= 229368, at[0]

    def slot(name, first, n, dt=F32):
        return place(name, [P, n, T], dt, WORK + first * SLOT)

    par_st = place("par_st", [P, NBK, P], F32, WORK)
    x_st = place("x_st", [P, QB, D], F32, WORK + 12288)
    xs_st = place("xs_st", [NS, D], F32, WORK + 12288 + 16384)
    rst = place("rst", [P, 2, P], F32, TMP)
    sqb = slot("sqb", 0, 8)
    cst = slot("cst", 8, 8)
    qT = slot("qT", 8, 8)
    kT = slot("kT", 30, 8)
    vtok = [place("v01", [P, 2, D], F32, WORK + 18 * SLOT), place("v23", [P, 2, D], F32, WORK + 40 * SLOT)]
    qk = place("qk", [P, DC, NS], F32, sto_at + 512)
    sc = place("sc", [P, NS * NPG + 1, NH], F32, WORK + 16 * SLOT)
    lfb = place("lfb", [P, NS * NPG, NH], F32, WORK + 38 * SLOT)
    pages = place("pages", [P, 4, D], F32, XG + DC * SLOT)
    k_pages2 = place("k_pages2", [P, 4, D], F32, XG + 2 * DC * SLOT)
    v_pages = [pages[:, i:i + 1, :] for i in range(4)]
    for i, first in enumerate((30, 32, 34, 36, 8, 10, 12, 14, 18, 20, 40, 42)):
        v_pages.append(place(f"v_page{i}", [P, 1, D], F32, WORK + first * SLOT)[:, :, :])
    VR = len(v_pages)
    qb = place("qb", [P, 2, D], F32, XG)
    ztok = place("ztok", [P, D], F32, XG + 8192)
    kst = place("kst", [P, D], F32, XG + 12288)
    negc = place("negc", [P, SEQ], F32R, TMP)
    nmax = place("nmax", [P, QB * NH], F32, TMP + 3 * SLOT + 32)
    rsum = place("rsum", [P, QB * NH], F32, TMP + 3 * SLOT + 32 + 256)
    rinv = place("rinv", [P, NH], F32, TMP + 3 * SLOT + 32 + 512)
    lftok = place("lftok", [P, QB + 1, NH], F32, TMP + 3 * SLOT + 32 + 640)
    smal = place("smal", [P, 2], F32, TMP + 3 * SLOT + 32 + 960)
    qh = place("qh", [P, DC, NS], F32R, sto_at)
    ql = place("ql", [P, DC, NS], F32R, sto_at + 256)
    osb = place("osb", [P, D], F32, TMP + 4 * SLOT + 32)
    sm = place("sm", [P, 6, P], F32, TMP + 6 * SLOT + 32)
    lfT = place("lfT", [NH, T], F32, TMP + 7 * SLOT + 32)
    gate = slot("gate", 0, LC)
    la = slot("la", LC, 5)
    xc = slot("xc", 22, LC)
    lb = slot("lb", LC + 5, 5)
    band_at = {(half, i): WORK + 32 * SLOT + (2 * half + i) * TILES * 4 * P for half in range(2) for i in range(2)}
    band_at[1, 1] = pt_at
    band = {(half, i): place(f"band{half}{i}", [P, TILES * P], F32, band_at[half, i])
            for half in range(2) for i in range(2)}
    lsp = place("lsp", [P, 8, LC], F32, WORK + 20 * SLOT)
    hst = place("hst", [P, 9, LC], F32, WORK + 20 * SLOT + 512)
    y_st = place("y_st", [P, 2, D], F32, WORK)

    psum = ExitStack()
    lin = [psum.enter_context(nc.psum_tensor(f"lin{i}", [P, 2, 512], F32)) for i in range(2)]
    aux = psum.enter_context(nc.psum_tensor("aux", [P, 2, 512], F32))
    aux2 = psum.enter_context(nc.psum_tensor("aux2", [P, 2, 512], F32))

    def sems(names):
        return [psum.enter_context(nc.semaphore(n)) for n in names.split()]

    raw_landed = sems("raw_landed0 raw_landed1")
    hi_ready, lo_ready, unit_done, out_free = sems("hi_ready lo_ready unit_done out_free")
    x_landed, par_landed, small_landed, consts = sems("x_landed par_landed small_landed consts")
    filled, fill_free, x_in, copies = sems("filled fill_free x_in copies")
    xh_ready, xg_ready, sq_ready, acc_ready = sems("xh_ready xg_ready sq_ready acc_ready")
    ssq_ready, root_ready, rstd_ready = sems("ssq_ready root_ready rstd_ready")
    pad_zero, sadd_ready, sadd_step, y_ready = sems("pad_zero sadd_ready sadd_step y_ready")
    ffn_tap, sc_tap, lru_tap, conv_ready, state_kept = sems("ffn_tap sc_tap lru_tap conv_ready state_kept")
    silu_ready, scaled_ready, c_scaled, conv_scaled = sems("silu_ready scaled_ready c_scaled conv_scaled")
    z_hi, z_lo = sems("z_hi z_lo")
    rows_T, rows_copied, rows_out = sems("rows_T rows_copied rows_out")
    head_sq, head_sum, head_root, head_recip, normed = sems("head_sq head_sum head_root head_recip normed")
    v_T, v_copied, v_out, k_out = sems("v_T v_copied v_out k_out")
    lf_pe, lf_act, lf_dve, lf_rows, lf_landed, lf_out = sems("lf_pe lf_act lf_dve lf_rows lf_landed lf_out")
    suffix, suffix_in = sems("suffix suffix_in")
    s_ready, max_ready, exp_ready = sems("s_ready max_ready exp_ready")
    pT_ready, pT_copied, pv_done = sems("pT_ready pT_copied pv_done")
    zt_step, zt_ready, zT_hi = sems("zt_step zt_ready zT_hi")
    b67_filled, b67_free, qb_ready = sems("b67_filled b67_free qb_ready")
    page_landed = sems("page0 page1 page2 page3 page4 page5 page6 page7")
    qh_ready, ql_ready = sems("qh_ready ql_ready")
    v_landed = sems(" ".join(f"v_page{i}_landed" for i in range(VR)))
    k_mult3 = sems("k_mult3")[0]
    k_mult, k_reduced, v_used, v_sum = sems("k_mult k_reduced v_used v_sum")
    sm_dve, sm_pe, sm_act = sems("sm_dve sm_pe sm_act")
    qk_ready, osb_ready, o_T, o_hi, zs_ready = sems("qk_ready osb_ready o_T o_hi zs_ready")
    lsp_act, lsp_dve, gelu_ready, xb_ready = sems("lsp_act lsp_dve gelu_ready xb_ready")
    band_zero, gate_ready, lru_ix = sems("band_zero gate_ready lru_ix")
    band_landed = sems("band_landed0 band_landed1")
    lru_th, lru_ex, lru_q, lru_root = sems("lru_th lru_ex lru_q lru_root")
    lru_sq, lru_b, lru_s, lru_h, lru_zt, h_kept = sems("lru_sq lru_b lru_s lru_h lru_zt h_kept")
    yT_ready, yT_copied = sems("yT_ready yT_copied")
    y_out = sems("y_out0 y_out1")
    block = psum.enter_context(nc.Block())

    def above_zero(value):
        return not isinstance(value, int) or value > 0

    def pair(ap):
        return ap[:, :, 0:TH]

    def two(ap):
        if len(ap.shape) == 3:
            return ap.rearrange("p o (a b) -> p (o a) b", a=2)
        return ap.rearrange("p (a b) -> p a b", a=2)

    def at1(tile, m):
        return tile[:, ds(m, 1), :]

    def col(name, off):
        return par[:, ds(rows[name] + off, 1)]

    def loop(e, n, body, peel_first=True, peel_last=True):
        a = 1 if peel_first else 0
        b = n - 1 if peel_last else n
        if peel_first:
            body(0, True, False)
        if b - a > 1:
            with e.Fori(a, b) as i:
                body(i, False, False)
        elif b - a == 1:
            body(a, False, False)
        if peel_last:
            body(n - 1, False, True)

    conv0 = {}
    n_ = 0
    for name, k in (("sc0", DC), ("ffn0", FC), ("ffn1", FC), ("lru", LC), ("ffn2", FC), ("sc1", DC), ("ffn3", FC)):
        conv0[name] = n_
        n_ += k
    NORMS = 2 * DEPTH

    def gcol(n, m):
        return col("ffn_norm" if n % 2 else "mix_norm", (n // 2) * DC + m)


    B67 = [(0, "qb", 0), (2, "ko", 0), (4, "ko", 1), (6, "qb", 1), (8, "ko", 2), (10, "ko", 3), (12, "ko", 4), (16, "qb", 2),
           (20, "zT", 0), (26, "qb", 3), (35, "qb", 4), (37, "zT", 1), (43, "qb", 5), (50, "qb", 6), (53, "zT", 2),
           (56, "qb", 7), (66, "zT", 3)]
    STEPS = QB * NH

    def b67_before(n):
        if n == 0:
            return b67_free, 0
        kinds = [k for _, k, _ in B67[:n]]
        q = kinds.count("qb")
        return (qb_ready, q) if kinds[-1] == "qb" else (b67_free, n - q)

    NPAGES = NS * NPG
    cost = [(t // NH + 1) + 1 + 1.5 * sum(s == t for s, _, _ in B67) for t in range(STEPS)]

    def pages_by(t):
        return 0 if t < 1 else NPAGES if t >= STEPS else max(0, int((NPAGES + 4) * sum(cost[:t + 1]) / sum(cost)) - 4)

    def pool_pages(n):
        return n - n // 4

    WARM = (3, 2, 2, 0)
    kv = [(b, h) for b in range(QB) for h in range(NH)]
    squares = [tsq, tz]
    pt_ring = [tsq, tz]
    p_ring = [ty, tsl]
    psf = {"S": [lin[0][:, 0, :], lin[0][:, 1, :]], "PT": [lin[1][:, 0, :], lin[1][:, 1, :]]}

    def flat2(ps):
        return ps[:, :, :].rearrange("p a b -> p (a b)")

    def state_rows(kind, j):
        if kind == "ffn":
            q = FC * 5
            pr = O["new_ffn_conv_prompt"][j].rearrange("b r (c p) -> (b r c) p", p=P)
            sm_ = O["new_ffn_conv_sample"][j].rearrange("s r (c p) -> s r c p", p=P)
            moves = [(pr, 0, 0, 2 * FC)]
            moves += [(sm_[s, 1], (2 + s) // 5, ((2 + s) % 5) * FC, FC) for s in range(NS)]
            return [q, q], moves
        if kind == "sc":
            pr = O["new_sconv_prompt"][j].rearrange("b r (c p) -> (b r c) p", p=P)
            sm_ = O["new_sconv_sample"][j].rearrange("s r (c p) -> s r c p", p=P)
            return [10 * DC], [(pr, 0, 0, 2 * DC)] + [(sm_[s, 1], 0, (2 + s) * DC, DC) for s in range(NS)]
        pr = O["new_lru_conv_prompt"][j].rearrange("b r (c p) -> (b r c) p", p=P)
        sm_ = O["new_lru_conv_sample"][j].rearrange("s r (c p) -> s r c p", p=P)
        return [11 * LC], [(pr, 0, 0, 3 * LC)] + [(sm_[s, 2], 0, (3 + s) * LC, LC) for s in range(NS)]

    STATES = [("sc", 0), ("ffn", 0), ("ffn", 1), ("lru", 0), ("ffn", 2), ("sc", 1), ("ffn", 3)]
    states_of = {"b0": 0, "dn0": 1, "dn1": 2, "lo": 3, "dn2": 4, "b1": 5, "dn3": 6}
    rows_dmas = [0]
    for kind, j in STATES:
        rows_dmas.append(rows_dmas[-1] + len(state_rows(kind, j)[1]))

    pieces = []
    for b in range(8):
        r = LB * b
        while r < LB * (b + 1):
            n = min(LB * (b + 1), (r // P + 1) * P) - r
            pieces.append((r // P, r % P, b, r - LB * b, n))
            r += n

    def sources(m):
        lo = LB * (P * m // LB)
        hi = LB * -(-P * (m + 1) // LB)
        return list(range(lo // P, -(-hi // P)))

    tile_at = {}
    for c in range(5):
        for m in range(5):
            if c in sources(m):
                tile_at[c, m] = len(tile_at)
    assert len(tile_at) == TILES

    @block.sync
    def _(sp):
        def load(seg, it, p):
            u = seg.u0 + 2 * it + p
            if above_zero(u - 1):
                sp.wait_ge(lo_ready, u - 1)
            name = seg.name
            if name.startswith("gu"):
                w = I["ffn_w_up" if p else "ffn_w_gate"][int(name[2])].rearrange("(k p) n -> p k n", p=P)
                src = w[:, :, ds(it * P, P)]
            elif name.startswith("dn"):
                w = I["ffn_w_down"][int(name[2])].rearrange("(k p) n -> p k n", p=P)
                src = w[:, p * KH:(p + 1) * KH, ds(it * P, P)]
            else:
                w, c0 = gsrc(name)
                src = w[:, :, ds(it * 2 * P + (c0 + p * P), P)]
            sp.dma_start(wraw[:, p, 0:seg.kt, :], src).then_inc(raw_landed[p], 16)

        def body(seg):
            def f(it, first, last):
                load(seg, it, 0)
                load(seg, it, 1)
            return f

        def page(cache, pt_index, dst, landed, free=None, uses=0):
            idx = sp.value_load(pt[0:1, ds(pt_index, 1)], min_val=0, max_val=NPOOL - 1)
            if free:
                sp.wait_ge(free, uses)
            sp.dma_start(dst, cache[0][ds(idx, 1)].rearrange("a p h d -> p a (h d)")).then_inc(landed, 16)

        def v_page(pt_index, i, free=None, uses=0):
            page(I["cache_v"], pt_index, v_pages[i], v_landed[i], free, uses)

        for seg in order:
            if seg.name == "c0":
                body(seg)(0, True, False)
                for b, blocks, r, n, src in plan[1::2]:
                    sp.dma_start(par_st[r:r + n, b:b + blocks, :], src).then_inc(par_landed, 16)
                with sp.Fori(1, seg.halves) as i:
                    body(seg)(i, False, False)
            elif seg.name == "wo":
                sp.wait_ge(small_landed, 16 * 8)
                sp.wait_ge(unit_done, segs["v"].u0 + 8)
                for g in range(8):
                    page(I["cache_k"], g, (pages, k_pages2)[g // 4][:, g % 4:g % 4 + 1, :], page_landed[g])
                with sp.Fori(1, NPAGES // 8) as i:
                    for g in range(8):
                        page(I["cache_k"], 8 * i + g, (pages, k_pages2)[g // 4][:, g % 4:g % 4 + 1, :], page_landed[g],
                             k_reduced, 8 * i + (g - 7))
                sp.wait_ge(k_reduced, NPAGES - 4)
                for i in range(2 * VR):
                    if i == 4:
                        sp.wait_ge(k_reduced, NPAGES)
                        body(seg)(0, True, False)
                        sp.wait_ge(pv_done, STEPS)
                    if i < VR:
                        v_page(i % 4 * NPG + i // 4, i)
                    else:
                        v_page(i % 4 * NPG + i // 4, i - VR, v_used, i - VR + 1)
                with sp.Fori(0, 2) as i:
                    for n in range(VR):
                        v_page(VR // 4 * i + ((4 + n % 4) * NPG + n // 4), n, v_used, VR * i + (VR + n + 1))
                with sp.Fori(1, seg.halves) as i:
                    body(seg)(i, False, False)
            elif seg.name == "lx":
                blocks = [(half, i, *piece) for half in range(2) for i in range(2) for piece in pieces]
                n = -(-len(blocks) // (seg.halves - 1))
                body(seg)(0, True, False)
                for it in range(1, seg.halves):
                    body(seg)(it, False, False)
                    if it == 1:
                        sp.wait_ge(band_zero, 4)
                    for half, i, c, r0, b, br, rows_ in blocks[n * (it - 1):n * it]:
                        w = I["lru_w_i" if i else "lru_w_a"][0, 8 * half + b, br:br + rows_, :]
                        m0 = min(m for m in range(5) if (c, m) in tile_at)
                        off = P * tile_at[c, m0] + LB * b - P * m0
                        sp.dma_start(band[half, i][r0:r0 + rows_, off:off + LB], w).then_inc(band_landed[half], 16)
            else:
                loop(sp, seg.halves, body(seg), peel_first=seg.u0 == 0, peel_last=False)

    @block.tensor
    def _(pe):
        mm = nc.tensor.matmul

        def unit(u, p, kt, ps, g, rhs_h, rhs_l, k0, start, stop, ready):
            pe.wait_ge(lo_ready, u + 1)
            if start:
                if above_zero(g - 1):
                    pe.wait_ge(out_free, g - 1)
            for k in range(kt):
                ready(k0 + k)
                for w, r in ((whi, rhs_h), (whi, rhs_l), (wlo, rhs_h)):
                    for half in range(2):
                        last = mm(ps[:, half, 0:TH], w[:, p, k, :], r[:, k0 + k, half * TH:(half + 1) * TH],
                                  start=start and k == 0 and w is whi and r is rhs_h,
                                  stop=stop and k == kt - 1 and w is wlo)
            last.then_inc(unit_done, 1)

        def norm_sum(n):
            pe.wait_ge(acc_ready, 9 * n + 9)
            for half in range(2):
                last = mm(aux[:, half, 0:TH], ones[:, :], acc[:, half * TH:(half + 1) * TH], start=True, stop=True)
            last.then_inc(ssq_ready, 1)

        def state_T(j):
            kind, lay = STATES[j]
            widths, _ = state_rows(kind, lay)
            name = {"sc": f"sc{lay}", "ffn": f"ffn{lay}", "lru": "lru"}[kind]
            pe.wait_ge(state_kept, conv0[name] + {"sc": DC, "ffn": FC, "lru": LC}[kind])
            for i, w in enumerate(widths):
                last = nc.tensor.transpose(aux2[0:w, i, 0:P], sto[:, i * w:(i + 1) * w], ident[:, :])
            if kind == "lru":
                pe.wait_ge(h_kept, LC)
                last = nc.tensor.transpose(aux2[0:9 * LC, 1, 0:P], hst[:, :, :].rearrange("p q c -> p (q c)"), ident[:, :])
            last.then_inc(rows_T, 1)

        def project(seg, norm=None, ready=None, extra=None):
            rh, rl = (xh, xl) if ready is None else (hh, hl)
            n_in = None if ready else norm_of(seg)

            def normed_input(k):
                pe.wait_ge(xg_ready, DC * n_in + k + 1)
            rd = ready or normed_input

            def body(it, first, last):
                for p in range(2):
                    u = seg.u0 + 2 * it + p
                    unit(u, p, seg.kt, lin[p], seg.g0 + 2 * it + p, rh, rl, 0, True, True, rd)
                    if first and p == 0 and norm is not None:
                        norm_sum(norm)
                    if first and p == 0 and seg.name in states_of and seg.name != "b0" and seg.name != "b1":
                        state_T(states_of[seg.name])
                    if extra:
                        extra(2 * it + p, first and p == 0)
                if first and seg.name in ("b0", "b1"):
                    state_T(states_of[seg.name])
            loop(pe, seg.halves, body, peel_last=False)

        def norm_of(seg):
            return {"c0": 0, "h0": 0, "b0": 0, "gu0": 1, "q": 2, "k": 2, "v": 2, "gu1": 3, "lx": 4, "lgA": 4, "lgB": 4, "gu2": 5,
                    "c1": 6, "h1": 6, "b1": 6, "gu3": 7}[seg.name]

        def down(l):
            seg = segs[f"dn{l}"]
            z0 = conv0[f"ffn{l}"]

            def rd(k):
                if k == 0:
                    pe.wait_ge(z_lo, z0 + KH)
                elif k == KH:
                    pe.wait_ge(z_lo, z0 + FC)

            def body(i2, first, last):
                for a in range(2):
                    for p in range(2):
                        u = seg.u0 + 4 * i2 + 2 * a + p
                        unit(u, p, KH, lin[a], seg.g0 + 2 * i2 + a, hh, hl, p * KH, p == 0, p == 1, rd)
                    if first and a == 0:
                        state_T(states_of[seg.name])
            loop(pe, DC // 2, body, peel_last=False)

        fills = [("par", f) for f in range(-(-NBK // 4))] + [("xs", 0)] + [("x", c) for c in range(DC)]
        nsmall = len(fills) - DC
        pe.wait_ge(consts, 1)
        pe.wait_ge(par_landed, 16 * len(plan))
        for i, (what, j) in enumerate(fills):
            bank = (aux, aux2)[(i % 4) // 2][:, i % 2, :]
            if i >= 4:
                if i - 4 < nsmall:
                    pe.wait_ge(fill_free, i - 3)
                else:
                    pe.wait_ge(x_in, i - 3 - nsmall)
            if what == "xs":
                pe.wait_ge(x_landed, 32)
            if what == "par":
                for b in range(4 * j, min(4 * j + 4, NBK)):
                    n = min(P, nrows - b * P)
                    last = nc.tensor.transpose(bank[:, (b % 4) * P:(b % 4) * P + n], par_st[0:n, b, :], ident[0:n, 0:n])
            elif what == "xs":
                for c in range(DC):
                    last = nc.tensor.transpose(bank[:, c * NS:(c + 1) * NS], xs_st[:, c * P:(c + 1) * P], ident[0:NS, 0:NS])
            else:
                for t in range(QB):
                    last = nc.tensor.transpose(bank[:, t * P:(t + 1) * P], x_st[:, t, j * P:(j + 1) * P], ident[:, :])
            last.then_inc(filled, 1)

        def short_conv(j, n):
            project(segs[f"c{j}"], norm=n)
            project(segs[f"h{j}"])
            project(segs[f"b{j}"])
            project(segs[f"so{j}"], ready=lambda k: pe.wait_ge(z_lo, conv0[f"sc{j}"] + k + 1))

        def ffn(l):
            project(segs[f"gu{l}"], norm=2 * l + 1)
            down(l)

        short_conv(0, 0)
        ffn(0)

        project(segs["q"], norm=2)
        pe.wait_ge(small_landed, 16 * 8)
        pe.wait_ge(rstd_ready, 3)
        for k in range(DC):
            for r in (xh, xl):
                for half in range(2):
                    last = mm(aux[0:NH, half, 0:TH], wf[:, k, :], r[:, k, half * TH:(half + 1) * TH].bitcast(F32),
                              start=k == 0 and r is xh, stop=k == DC - 1 and r is xl)
        last.then_inc(lf_pe, 1)

        def k_extra(m, first):
            if first:
                pe.wait_ge(lf_dve, 2)
            pe.wait_ge(head_sq, m + 1)
            if above_zero(m):
                pe.wait_ge(head_root, m)
            for half in range(2):
                last = mm(aux[:, half, 0:TH], blk[:, :], sq_chunk(m, half), start=True, stop=True)
            last.then_inc(head_sum, 1)

        def sq_chunk(m, half):
            return at1(sqb, m).rearrange("p o t -> p (o t)")[:, half * TH:(half + 1) * TH]

        def turn_v(m):
            pe.wait_ge(out_free, segs["v"].g0 + m + 1)
            if above_zero(m):
                pe.wait_ge(v_copied, m)
            for t in range(QB):
                nc.tensor.transpose(aux2[:, 0, t * P:(t + 1) * P], tt[:, t * P:(t + 1) * P], ident[:, :])
            nc.tensor.transpose(aux2[0:NS, 1, 0:P], tt[:, SEQ:T], ident[:, :]).then_inc(v_T, 1)

        def v_extra(m, first):
            pe.wait_ge(head_sq, DC + m + 1)
            pe.wait_ge(head_root, DC + m)
            for half in range(2):
                last = mm(aux[:, half, 0:TH], blk[:, :], sq_chunk(m, half), start=True, stop=True)
            last.then_inc(head_sum, 1)
            if not first:
                turn_v(m - 1)

        project(segs["k"], extra=k_extra)
        project(segs["v"], extra=v_extra)
        turn_v(DC - 1)

        pe.wait_ge(head_root, 2 * DC)
        pe.wait_ge(lf_dve, 10)
        for t in range(QB):
            nc.tensor.transpose(aux[:, 0, t * NH:(t + 1) * NH], lfT[0:NH, t * P:(t + 1) * P], ident[0:NH, 0:NH])
        nc.tensor.transpose(aux[0:NS, 0, QB * NH:(QB + 1) * NH], lfT[0:NH, SEQ:T], ident[0:NH, 0:NH]).then_inc(lf_rows, 1)
        pe.wait_ge(lf_landed, 16 * NS * NPG)
        for half in range(2):
            if half == 0:
                dst = aux[:, 1, :]
            else:
                dst = lin[0][:, 0, :]
                pe.wait_ge(out_free, segs["v"].g0 + DC)
            lf4 = lfb[:, half * 32:(half + 1) * 32, :].rearrange("p (s g) h -> p s (g h)", g=NPG)
            d4 = dst.rearrange("p (s n) -> p s n", s=4)
            mm(dst, tri[:, :], lfb[:, half * 32:(half + 1) * 32, :].rearrange("p a h -> p (a h)"), start=True, stop=False)
            for k in range(1, NPG):
                last = mm(d4[:, :, 0:(NPG - k) * NH], ones[:, :], lf4[:, :, k * NH:NPG * NH], start=False, stop=k == NPG - 1)
            last.then_inc(suffix, 1)

        pe.wait_ge(normed, 2 * DC)
        pe.wait_ge(lf_dve, 12)
        pe.wait_ge(suffix_in, 2)
        pe.wait_ge(v_copied, DC)
        items = {s: (k, i, n) for n, (s, k, i) in enumerate(B67)}
        pe.wait_ge(consts, 3)
        pe.wait_ge(ql_ready, 1)

        def item(step):
            if step not in items:
                return
            kind, i, n = items[step]
            before, uses = b67_before(n)
            if uses:
                pe.wait_ge(before, uses)
            dst = flat2(aux2)
            if kind == "qb":
                for c in range(DC):
                    mm(dst[:, c * P:(c + 1) * P], qh[:, c, i:i + 1].to_broadcast([P, P]), identr[:, :], start=True, stop=False)
                    last = mm(dst[:, c * P:(c + 1) * P], ql[:, c, i:i + 1].to_broadcast([P, P]), identr[:, :],
                              start=False, stop=True)
            elif kind == "ko":
                n_tok = P if i < QB else NS
                for c in range(DC):
                    last = nc.tensor.transpose(dst[0:n_tok, c * P:(c + 1) * P], kT[:, c, i * P:i * P + n_tok], ident[:, :])
            else:
                pe.wait_ge(zt_ready, 2 * (i + 1))
                for c in range(DC):
                    last = nc.tensor.transpose(dst[:, c * P:(c + 1) * P], ztok[:, c * P:(c + 1) * P], ident[:, :])
            last.then_inc(b67_filled, 1)

        for t in range(STEPS + 4):
            if t < STEPS:
                b, h = kv[t]
                w = (b + 1) * P
                r0 = HD * (h % 2)
                s_ps = psf["S"][t % 2]
                if above_zero(t - 1):
                    pe.wait_ge(exp_ready, t - 1)
                for _ in range(WARM[b]):
                    mm(s_ps[:, :], identr[:, :], negc[:, :], start=True, stop=True)
                mm(s_ps[:, 0:w], qT[r0:r0 + HD, h // 2, b * P:(b + 1) * P], kT[r0:r0 + HD, h // 2, 0:w], start=True, stop=False)
                mm(s_ps[:, 0:w], pick[:, h:h + 1].to_broadcast([P, P]), negc[:, 0:w], start=False, stop=False)
                mm(s_ps[:, 0:w], negc[:, b * P:(b + 1) * P], pickm[:, h:h + 1].to_broadcast([P, w]), start=False, stop=False)
                mm(s_ps[:, b * P:w], identr[:, :], maskr[:, :], start=False, stop=True).then_inc(s_ready, 1)
            if 2 <= t <= STEPS + 1:
                b, h = kv[t - 2]
                pe.wait_ge(exp_ready, t - 1)
                if above_zero(t - 3):
                    pe.wait_ge(pT_copied, t - 3)
                for j in range(b + 1):
                    last = nc.tensor.transpose(psf["PT"][t % 2][:, j * P:(j + 1) * P],
                                               p_ring[t % 2][:, j * P:(j + 1) * P], ident[:, :])
                last.then_inc(pT_ready, 1)
            if 3 <= t <= STEPS + 2:
                b, h = kv[t - 3]
                pe.wait_ge(pT_copied, t - 2)
                if h == 0 and b:
                    pe.wait_ge(zt_ready, 2 * b)
                for j in range(b + 1):
                    last = mm(flat2(aux)[:, h * HD:(h + 1) * HD], pt_ring[(t - 3) % 2][:, j * P:(j + 1) * P],
                              vtok[j // 2][:, j % 2, h * HD:(h + 1) * HD], start=j == 0, stop=j == b)
                last.then_inc(pv_done, 1)
            item(t)

        B2, B3 = lin[1][:, 0, :], lin[1][:, 1, :]
        pe.wait_ge(pT_copied, STEPS)
        pe.wait_ge(qk_ready, 1)
        for c in range(DC):
            last = mm(B2[0:NS, 2 * c:2 * c + 2], qk[:, c, :], blk[:, 0:P:HD], start=True, stop=True)
        last.then_inc(sm_pe, 1)
        pe.wait_ge(sm_dve, 2)
        mm(B2[:, P:2 * P], ones[0:NS, :], sm[0:NS, 1, :], start=True, stop=True)
        mm(B2[:, 2 * P:3 * P], ones[0:NS, :], sm[0:NS, 2, :], start=True, stop=True).then_inc(sm_pe, 1)
        pe.wait_ge(sm_dve, 6)
        nc.tensor.transpose(B3[:, 0:P], sm[:, 3, :], ident[:, :]).then_inc(sm_pe, 1)
        pe.wait_ge(sm_dve, 8)
        mm(B3[:, P:2 * P], ones[:, :], sm[:, 5, :], start=True, stop=True).then_inc(sm_pe, 1)
        pe.wait_ge(sm_dve, 13)
        mm(B3[:, 2 * P:3 * P], ones[:, :], sm[:, 5, :], start=True, stop=True).then_inc(sm_pe, 1)
        def sample_out(half):
            pe.wait_ge(osb_ready, half + 1)
            for c in range(DC):
                last = mm(B2[:, 384 + 32 * half + 4 * c:388 + 32 * half + 4 * c], osb[:, c * P:(c + 1) * P], jsel[:, :],
                          start=True, stop=True)
            last.then_inc(o_T, 1)

        pe.wait_ge(sm_dve, 17)
        before, uses = b67_before(len(B67))
        pe.wait_ge(before, uses)
        pe.wait_ge(zt_ready, 2 * QB)
        own = sm[0:NS, 3:5, :].rearrange("p a c -> p (a c)")
        for half in range(2):
            o = (aux, aux2)[half]
            for g in range(NPG):
                for j in range(4):
                    i = half * 4 * NPG + g * 4 + j
                    pe.wait_ge(v_landed[i % VR], 16 * (i // VR + 1))
                    for n in range(2):
                        page_ = (half * 4 + j) * NPG + g
                        last = mm(o[32 * j:32 * j + 32, n, :], sc[:, page_:page_ + 2, :].rearrange("p a h -> p (a h)"),
                                  v_pages[i % VR][:, 0, n * 512:(n + 1) * 512], start=g == 0, stop=False)
                    last.then_inc(v_used, 1)
                if half == 1 and g == 3:
                    sample_out(0)
            for j in range(4):
                for n in range(2):
                    last = mm(o[32 * j:32 * j + 32, n, :], own[:, (half * 4 + j) * NH:(half * 4 + j) * NH + 32],
                              vsr[:, n * 512:(n + 1) * 512], start=False, stop=True)
            last.then_inc(v_sum, 1)
        sample_out(1)

        pe.wait_ge(zs_ready, 2)
        project(segs["wo"], ready=lambda k: None)
        ffn(1)

        def gates(hf):
            seg = segs[f"gates{hf}"]
            pe.wait_ge(band_landed[hf], 16 * 2 * len(pieces))
            for m in range(5):
                for i in range(2):
                    g = seg.g0 + 2 * m + i
                    pe.wait_ge(out_free, g - 1)
                    cs = sources(m)
                    for c in cs:
                        pe.wait_ge(conv_ready, conv0["lru"] + 5 * hf + c + 1)
                        for half in range(2):
                            last = mm(lin[i][:, half, 0:TH], band[hf, i][:, P * tile_at[c, m]:P * (tile_at[c, m] + 1)],
                                      xc[:, 5 * hf + c, half * TH:(half + 1) * TH], start=c == cs[0], stop=c == cs[-1])
                    last.then_inc(gate_ready, 1)

        project(segs["lx"], norm=4)
        gates(0)
        project(segs["lgA"])
        gates(1)
        project(segs["lgB"])
        project(segs["lo"], ready=lambda k: pe.wait_ge(z_lo, conv0["lru"] + k + 1))
        ffn(2)
        short_conv(1, 6)
        ffn(3)

        for t in range(QB + 1):
            n_tok = P if t < QB else NS
            pe.wait_ge(out_free, segs["dn3"].g0 + DC)
            if above_zero(t - 1):
                pe.wait_ge(yT_copied, t - 1)
            for c in range(DC):
                last = nc.tensor.transpose(flat2(lin[t % 2])[0:n_tok, c * P:(c + 1) * P], x[:, c, t * P:t * P + n_tok],
                                           ident[:, :])
            last.then_inc(yT_ready, 1)

    @block.scalar
    def _(act):
        A = nc.scalar.activation

        def split(u, p, kt):
            act.wait_ge(raw_landed[p], (u - p) * 8 + 16)
            if above_zero(u - 1):
                act.wait_ge(unit_done, u - 1)
            nc.scalar.copy(whi[:, p, 0:kt, :], wraw[:, p, 0:kt, :]).then_inc(hi_ready, 1)

        def split_next(seg, it, p, last):
            kt = seg.next_kt if last else seg.kt
            if kt:
                split(seg.u0 + 2 * it + p + 2, p, kt)

        def root(n):
            act.wait_ge(ssq_ready, n + 1)
            A(two(rstd[:, :]), pair(aux), ACT.Sqrt, bias=eps[:, 0:1], scale=1.0 / D).then_inc(root_ready, 1)

        def prep(n, m, p, x_new, value):
            act.wait_ge(acc_ready, 9 * n + m if above_zero(9 * n + m) else 1)
            act.wait_ge(x_new, value)
            A(at1(xh, m), at1(x, m), ACT.Copy, scale=gcol(n, m)).then_inc(xh_ready, 1)
            A(squares[p][:, :], at1(x, m).rearrange("p o t -> p (o t)"), ACT.Square).then_inc(sq_ready, 1)

        def rows_move(j):
            kind, lay = STATES[j]
            widths, moves = state_rows(kind, lay)
            act.wait_ge(rows_T, j + 1)
            for i, w in enumerate(widths):
                nc.scalar.copy(rst[0:w, i, :], aux2[0:w, i, 0:P]).then_inc(rows_copied, 1)
            if kind == "lru":
                nc.scalar.copy(rst[0:9 * LC, 1, :], aux2[0:9 * LC, 1, 0:P]).then_inc(rows_copied, 1)
            act.wait_ge(rows_copied, copied[j + 1])
            for dst, part, r, n in moves:
                act.dma_start(dst, rst[r:r + n, part, :]).then_inc(rows_out, 16)
            if kind == "lru":
                act.dma_start(O["new_lru_h_prompt"][0].rearrange("b (c p) -> (b c) p", p=P), rst[0:LC, 1, :]
                              ).then_inc(rows_out, 16)
                act.dma_start(O["new_lru_h_sample"][0].rearrange("s (c p) -> (s c) p", p=P), rst[LC:9 * LC, 1, :]
                              ).then_inc(rows_out, 16)

        def seg_loop(seg, epilogue, norm=None, states=None):
            def body(it, first, last):
                for p in range(2):
                    split_next(seg, it, p, last)
                    if first and p == 0 and norm is not None:
                        root(norm)
                    epilogue(2 * it + p, seg.g0 + 2 * it + p, p)
                    if first and p == 1 and states is not None:
                        rows_move(states)
            loop(act, seg.halves, body)

        def conv_tap(V, w_last, b=None, off=2):
            if above_zero(V):
                act.wait_ge(conv_ready, V)
            A(ty[:, :], ext[:, off:off + T], ACT.Identity, scale=w_last, bias=0.0 if b is None else b
              ).then_inc(y_ready, 1)

        def out_proj(name, n):
            seg = segs[name]
            seg_loop(seg, lambda m, g, p: prep(n, m, p, out_free, g + 1), states=states_of.get(name))

        def short_conv(j, n):
            v0 = conv0[f"sc{j}"]
            seg_loop(segs[f"c{j}"], lambda m, g, p: None, norm=n)

            def h_ep(m, g, p):
                act.wait_ge(out_free, g + 1)
                conv_tap(v0 + m, col("sc_conv_w", j * 3 * DC + 2 * DC + m))
            seg_loop(segs[f"h{j}"], h_ep)

            def b_ep(m, g, p):
                act.wait_ge(out_free, g + 1)
                nc.scalar.copy(at1(hh, m), tt[:, :].unsqueeze(1)).then_inc(z_hi, 1)
            seg_loop(segs[f"b{j}"], b_ep, states=states_of[f"b{j}"])
            out_proj(f"so{j}", n + 1)

        def ffn(l):
            seg, v0 = segs[f"gu{l}"], conv0[f"ffn{l}"]

            def body(it, first, last):
                g, V = seg.g0 + 2 * it, v0 + it
                split_next(seg, it, 0, last)
                if first:
                    root(2 * l + 1)
                    if l == 1:
                        act.wait_ge(v_out, 16 * (QB // 2 + 1))
                act.wait_ge(out_free, g + 1)
                if above_zero(l * FC + it):
                    act.wait_ge(silu_ready, l * FC + it)
                conv_tap(V, col("ffn_conv_w", l * 3 * FC + 2 * FC + it), col("ffn_conv_b", l * FC + it))
                split_next(seg, it, 1, last)
                act.wait_ge(conv_ready, V + 1)
                act.wait_ge(out_free, g)
                A(tsl[:, :], ty[:, :], ACT.Silu).then_inc(silu_ready, 1)
                act.wait_ge(out_free, g + 2)
                nc.scalar.copy(at1(hh, it), tt[:, :].unsqueeze(1)).then_inc(z_hi, 1)
            loop(act, seg.halves, body)

            seg2 = segs[f"dn{l}"]
            n = 2 * l + 2

            def body2(i2, first, last):
                for a in range(2):
                    for p in range(2):
                        if not (last and a == 1):
                            split(seg2.u0 + 4 * i2 + 2 * a + p + 2, p, KH)
                        elif seg2.next_kt:
                            split(seg2.u0 + 4 * i2 + 2 * a + p + 2, p, seg2.next_kt)
                    if n < NORMS:
                        prep(n, 2 * i2 + a, a, out_free, seg2.g0 + 2 * i2 + a + 1)
                    if first and a == 0:
                        rows_move(states_of[f"dn{l}"])
            loop(act, DC // 2, body2)

        copied = [0]
        for kind, lay in STATES:
            copied.append(copied[-1] + len(state_rows(kind, lay)[0]) + (kind == "lru"))

        act.dma_start(x_st[:, :, :], I["x_prompt"][0].rearrange("(t p) d -> p t d", p=P)).then_inc(x_landed, 16)
        act.dma_start(xs_st[:, :], I["x_sample"].rearrange("s t d -> (s t) d")).then_inc(x_landed, 16)
        for b, blocks, r, n, src in plan[::2]:
            act.dma_start(par_st[r:r + n, b:b + blocks, :], src).then_inc(par_landed, 16)
        split(0, 0, 8)
        split(1, 1, 8)
        act.wait_ge(consts, 3)
        for m in range(DC):
            prep(0, m, m % 2, x_in, m + 1)

        short_conv(0, 0)
        ffn(0)

        def square(m, src, value, g):
            act.wait_ge(out_free, g)
            if value:
                act.wait_ge(head_sum, m + 1)
            A(at1(sqb, m), at1(src, m), ACT.Square).then_inc(head_sq, 1)

        def head_sqrt(i):
            act.wait_ge(head_sum, i + 1)
            if above_zero(i):
                act.wait_ge(normed, i)
            A(two(ty[:, :]), pair(aux), ACT.Sqrt, bias=eps[:, 0:1], scale=1.0 / HD).then_inc(head_root, 1)

        seg_loop(segs["q"], lambda m, g, p: square(m, qT, 0, g + 1), norm=2)
        act.wait_ge(lf_dve, 4)
        A(tsl[0:NH, :], ty[0:NH, :], ACT.Exp, scale=-1.0).then_inc(lf_act, 1)
        act.wait_ge(lf_dve, 5)
        A(ty[0:NH, :], tsq[0:NH, :], ACT.Ln).then_inc(lf_act, 1)
        act.wait_ge(lf_dve, 11)
        A(negc[0:NH, :], tt[0:NH, 0:SEQ], ACT.Copy, scale=-1.0).then_inc(lf_act, 1)

        def k_ep(m, g, p):
            head_sqrt(m)
            square(m, kT, 1, g + 1)
        seg_loop(segs["k"], k_ep)

        act.wait_ge(normed, DC)
        nc.scalar.copy(qh[:, :, :], qT[:, :, SEQ:T]).then_inc(qh_ready, 1)

        def v_copy(m):
            act.wait_ge(v_T, m + 1)
            for i in range(2):
                nc.scalar.copy(vtok[i][:, :, ds(m * P, P)], aux2[:, 0, i * 256:(i + 1) * 256].rearrange("p (t d) -> p t d", t=2))
            nc.scalar.copy(vsr[:, ds(m * P, P)], aux2[0:NS, 1, 0:P]).then_inc(v_copied, 1)

        seg = segs["v"]

        def v_body(it, first, last):
            for p in range(2):
                m = 2 * it + p
                split_next(seg, it, p, last)
                head_sqrt(DC + m)
                if not (first and p == 0):
                    v_copy(m - 1)
        loop(act, seg.halves, v_body)
        v_copy(DC - 1)
        act.wait_ge(v_copied, DC)
        for i in range(2):
            act.dma_start(O["new_v_prompt"][0, 0, i * 256:(i + 1) * 256].rearrange("(t p) h d -> p t (h d)", p=P), vtok[i][:, :, :]
                          ).then_inc(v_out, 16)
        act.dma_start(O["new_v_sample"][0].rearrange("s t h d -> (s t) (h d)"), vsr[:, :]).then_inc(v_out, 16)
        act.wait_ge(lf_rows, 2)
        act.dma_start(O["new_logf_prompt"][0, 0].rearrange("(t p) h -> p t h", p=P), lftok[:, 0:QB, :]).then_inc(lf_out, 16)
        act.dma_start(O["new_logf_sample"][0].rearrange("s t h -> (s t) h"), lftok[0:NS, QB, :]).then_inc(lf_out, 16)

        done = {s + 1: (k, i, n) for n, (s, k, i) in enumerate(B67)}
        for t in range(STEPS + 4):
            if t < STEPS:
                b, h = kv[t]
                w = (b + 1) * P
                act.wait_ge(max_ready, t + 1)
                if above_zero(t - 1):
                    act.wait_ge(pT_ready, t - 1)
                A(p_ring[t % 2][:, 0:w], psf["S"][t % 2][:, 0:w], ACT.Exp, bias=nmax[:, t:t + 1],
                  accum_out=rsum[:, t:t + 1]).then_inc(exp_ready, 1)
            if 2 <= t <= STEPS + 1:
                b, h = kv[t - 2]
                w = (b + 1) * P
                act.wait_ge(pT_ready, t - 1)
                if above_zero(t - 3):
                    act.wait_ge(pv_done, t - 3)
                nc.scalar.copy(pt_ring[t % 2][:, 0:w], psf["PT"][t % 2][:, 0:w]).then_inc(pT_copied, 1)
            if t in done:
                kind, i, n = done[t]
                act.wait_ge(b67_filled, n + 1)
                if kind == "qb":
                    if i >= 2:
                        act.wait_ge(k_mult, pool_pages(NPG * (i - 1)))
                        act.wait_ge(k_mult3, NPG * (i - 1) // 4)
                    nc.scalar.copy(qb[:, i % 2, :], flat2(aux2)).then_inc(qb_ready, 1)
                elif kind == "ko":
                    n_tok = P if i < QB else NS
                    if above_zero(16 * i):
                        act.wait_ge(k_out, 16 * i)
                    nc.scalar.copy(kst[0:n_tok, :], flat2(aux2)[0:n_tok, :]).then_inc(b67_free, 1)
                    copied_k, uses = b67_before(n + 1)
                    act.wait_ge(copied_k, uses)
                    if i < QB:
                        dst = O["new_k_prompt"][0, 0, i * P:(i + 1) * P].rearrange("t h d -> t (h d)")
                    else:
                        dst = O["new_k_sample"][0].rearrange("s t h d -> (s t) (h d)")
                    act.dma_start(dst, kst[0:n_tok, :]).then_inc(k_out, 16)
                else:
                    nc.scalar.copy(hh[:, 0:DC, i * P:(i + 1) * P], flat2(aux2).rearrange("p (c t) -> p c t", c=DC)
                                   ).then_inc(zT_hi, 1)
        act.wait_ge(sm_dve, 11)
        A(sc[:, 0:NPAGES, :], sc[:, 0:NPAGES, :], ACT.Exp).then_inc(sm_act, 1)
        A(sm[:, 4, :], sm[:, 4, :], ACT.Exp).then_inc(sm_act, 1)
        split(segs["wo"].u0, 0, 8)
        split(segs["wo"].u0 + 1, 1, 8)
        for half in range(2):
            act.wait_ge(o_T, half + 1)
            nc.scalar.copy(hh[:, 0:DC, SEQ + 4 * half:SEQ + 4 * half + 4],
                           lin[1][:, 0, 384 + 32 * half:416 + 32 * half].rearrange("p (c s) -> p c s", c=DC)
                           ).then_inc(o_hi, 1)
        act.wait_ge(k_out, 16 * (QB + 1))
        out_proj("wo", 3)
        ffn(1)

        act.wait_ge(lsp_dve, 2)
        A(lsp[:, 2, :], lsp[:, 1, :], ACT.Exp, scale=-1.0).then_inc(lsp_act, 1)
        act.wait_ge(lsp_dve, 3)
        A(lsp[:, 4, :], lsp[:, 3, :], ACT.Ln).then_inc(lsp_act, 1)

        v0 = conv0["lru"]

        def lx_ep(m, g, p):
            act.wait_ge(out_free, g + 1)
            act.wait_ge(conv_ready, v0 + m)
            act.wait_ge(state_kept, v0 + m)
            act.wait_ge(y_ready, v0 + m)
            if isinstance(m, int) and m == 0:
                act.wait_ge(pad_zero, 4)
            A(ext[:, 3:3 + T], tt[:, :], ACT.Identity, bias=col("lru_b_in", LC + m)).then_inc(xb_ready, 1)
            act.wait_ge(xb_ready, m + 1)
            conv_tap(v0 + m, col("lru_conv_w", 3 * LC + m), col("lru_conv_b", m), off=3)
        seg_loop(segs["lx"], lx_ep, norm=4)

        def gates(hf):
            g0 = segs[f"gates{hf}"].g0
            for ms in ((0, 1, 2), (3, 4)):
                for m5 in ms:
                    m = 5 * hf + m5
                    act.wait_ge(gate_ready, 2 * m + 1)
                    if hf:
                        act.wait_ge(lru_h, m5 + 1)
                    A(two(la[:, m5, :]), pair(lin[0]), ACT.Sigmoid, bias=col("lru_b_a", m)).then_inc(out_free, 1)
                    act.wait_ge(gate_ready, 2 * m + 2)
                    A(two(lb[:, m5, :]), pair(lin[1]), ACT.Sigmoid, bias=col("lru_b_i", m)).then_inc(out_free, 1)
                    act.wait_ge(out_free, g0 + 2 * m5 + 1)
                    A(gate[:, m, :], la[:, m5, :], ACT.Tanh, scale=lsp[:, 7, m:m + 1]).then_inc(lru_th, 1)
                for m5 in ms:
                    m = 5 * hf + m5
                    act.wait_ge(lru_th, m + 1)
                    A(la[:, m5, :], la[:, m5, :], ACT.Exp, scale=lsp[:, 7, m:m + 1]).then_inc(lru_ex, 1)
            for m in range(5 * hf, 5 * hf + 5):
                act.wait_ge(lru_q, m + 1)
                act.wait_ge(lru_ix, m + 1)
                A(xc[:, m, :], gate[:, m, :], ACT.Sqrt, scale=-1.0).then_inc(lru_root, 1)

        def z_high(m):
            act.wait_ge(lru_zt, m + 1)
            nc.scalar.copy(hh[:, m, :], tz[:, :]).then_inc(z_hi, 1)

        def gate_branch(name, first_m):
            seg = segs[name]
            for i in range(seg.units):
                m = first_m + i
                split_next(seg, i // 2, i % 2, i // 2 == seg.halves - 1)
                if m:
                    z_high(m - 1)
                act.wait_ge(out_free, seg.g0 + i + 1)
                act.wait_ge(lru_root, m + 1)
                A(gate[:, m, :], tt[:, :], ACT.Gelu_apprx_tanh, bias=col("lru_b_in", m)).then_inc(gelu_ready, 1)

        gates(0)
        gate_branch("lgA", 0)
        gates(1)
        gate_branch("lgB", LGA)
        z_high(LC - 1)
        act.wait_ge(h_kept, LC)
        out_proj("lo", 5)
        ffn(2)
        short_conv(1, 6)
        ffn(3)

        for t in range(QB + 1):
            n_tok = P if t < QB else NS
            act.wait_ge(yT_ready, t + 1)
            if above_zero(16 * (t // 2)):
                act.wait_ge(y_out[t % 2], 16 * (t // 2))
            nc.scalar.copy(y_st[0:n_tok, t % 2, :], flat2(lin[t % 2])[0:n_tok, :]).then_inc(yT_copied, 1)
            act.wait_ge(yT_copied, t + 1)
            dst = O["y_prompt"][0, t * P:(t + 1) * P] if t < QB else O["y_sample"].rearrange("s t d -> (s t) d")
            act.dma_start(dst, y_st[0:n_tok, t % 2, :]).then_inc(y_out[t % 2], 16)
        act.wait_ge(y_out[0], 16 * (QB // 2 + 1))
        act.wait_ge(y_out[1], 16 * (QB // 2))
        act.wait_ge(rows_out, 16 * (rows_dmas[-1] + 2))
        act.wait_ge(k_out, 16 * (QB + 1))
        act.wait_ge(v_out, 16 * (QB // 2 + 1))
        act.wait_ge(lf_out, 32)
        act.wait_ge(copies, 32)
        act.wait_ge(small_landed, 16 * 8)

    @block.vector
    def _(dve):
        V_ = nc.vector
        TT, STT, TS = V_.tensor_tensor, V_.scalar_tensor_tensor, V_.tensor_scalar

        def split(u, p, kt):
            dve.wait_ge(hi_ready, u + 1)
            TT(wlo[:, p, 0:kt, :], wraw[:, p, 0:kt, :], whi[:, p, 0:kt, :].bitcast(F32), ALU.subtract
               ).then_inc(lo_ready, 1)

        def split_next(seg, it, p, last):
            kt = seg.next_kt if last else seg.kt
            if kt:
                split(seg.u0 + 2 * it + p + 2, p, kt)

        def root(n):
            dve.wait_ge(root_ready, n + 1)
            V_.reciprocal(rstd[:, :], rstd[:, :]).then_inc(rstd_ready, 1)
            dve.wait_ge(rstd_ready, n + 1)

        def prep(n, m):
            dve.wait_ge(xh_ready, DC * n + m + 1)
            STT(out=at1(xl, m), in0=at1(x, m), scalar=gcol(n, m), in1=at1(xh, m).bitcast(F32), op0=ALU.mult, op1=ALU.subtract
                ).then_inc(xg_ready, 1)

        def seg_loop(seg, epilogue, norm=None, evacuate=None):
            def body(it, first, last):
                for p in range(2):
                    early = evacuate and not (first and p == 0)
                    if not early:
                        split_next(seg, it, p, last)
                    if first and p == 0 and norm is not None:
                        root(norm)
                    dve.wait_ge(unit_done, seg.u0 + 2 * it + p + 1)
                    if evacuate:
                        evacuate(2 * it + p, lin[p])
                    if early:
                        split_next(seg, it, p, last)
                    epilogue(2 * it + p, seg.g0 + 2 * it + p, lin[p])
            loop(dve, seg.halves, body)

        def pads(which, phase):
            extra = 2 if which > 3 else 0
            if above_zero(16 * (rows_dmas[which] + extra)):
                dve.wait_ge(rows_out, 16 * (rows_dmas[which] + extra))
            V_.memset(ext[:, 0:3], 0.0).then_inc(pad_zero, 1)
            dve.wait_ge(pad_zero, phase)

        def out_proj(name, n):
            def ep(m, g, ps):
                TT(two(at1(x, m)), pair(ps), two(at1(x, m)), ALU.add).then_inc(out_free, 1)
                prep(n, m)
            seg_loop(segs[name], ep)

        def z_split(m, V):
            dve.wait_ge(z_hi, V + 1)
            TT(at1(hl, m), tt[:, :].unsqueeze(1), at1(hh, m).bitcast(F32), ALU.subtract).then_inc(z_lo, 1)

        def short_conv(j, n, which, phase):
            v0 = conv0[f"sc{j}"]
            pads(which, phase)

            def c_ep(m, g, ps):
                TT(two(at1(cst, m)), pair(ps), two(rstd[:, :]), ALU.mult).then_inc(out_free, 1)
            seg_loop(segs[f"c{j}"], c_ep, norm=n)

            def h_ep(m, g, ps):
                V = v0 + m
                dve.wait_ge(c_scaled, j * DC + m + 1)
                if above_zero(V):
                    dve.wait_ge(y_ready, V)
                if above_zero(V):
                    dve.wait_ge(conv_ready, V)
                if above_zero(V):
                    dve.wait_ge(state_kept, V)
                TT(two(ext[:, 2:2 + T]), pair(ps), two(at1(cst, m)), ALU.mult).then_inc(out_free, 1)
                dve.wait_ge(y_ready, V + 1)
                dve.wait_ge(out_free, g + 1)
                if isinstance(m, int) and m == 0:
                    dve.wait_ge(sadd_ready, phase)
                w0 = col("sc_conv_w", j * 3 * DC + m)
                w1 = col("sc_conv_w", j * 3 * DC + DC + m)
                STT(out=ty[:, 0:SEQ], in0=ext[:, 1:1 + SEQ], scalar=w1, in1=ty[:, 0:SEQ], op0=ALU.mult, op1=ALU.add
                    ).then_inc(sc_tap, 1)
                TT(cst[:, ds(m, 1), SEQ:T], ty[:, SEQ:T].unsqueeze(1), sadd[:, ds(m, 1), :], ALU.add).then_inc(sc_tap, 1)
                dve.wait_ge(sc_tap, 2 * (j * DC + m) + 2)
                STT(out=cst[:, ds(m, 1), 0:SEQ], in0=ext[:, 0:SEQ].unsqueeze(1), scalar=w0, in1=ty[:, 0:SEQ].unsqueeze(1),
                    op0=ALU.mult, op1=ALU.add).then_inc(conv_ready, 1)
            seg_loop(segs[f"h{j}"], h_ep)

            def b_ep(m, g, ps):
                V = v0 + m
                dve.wait_ge(conv_scaled, j * DC + m + 1)
                if above_zero(V):
                    dve.wait_ge(z_lo, V)
                TT(two(tt[:, :]), pair(ps), two(at1(cst, m)), ALU.mult).then_inc(out_free, 1)
                z_split(m, V)
            seg_loop(segs[f"b{j}"], b_ep)
            out_proj(f"so{j}", n + 1)

        def ffn(l, which, phase):
            seg, v0 = segs[f"gu{l}"], conv0[f"ffn{l}"]
            pads(which, phase)

            def body(it, first, last):
                g, V = seg.g0 + 2 * it, v0 + it
                split_next(seg, it, 0, last)
                if first:
                    root(2 * l + 1)
                dve.wait_ge(unit_done, seg.u0 + 2 * it + 1)
                dve.wait_ge(y_ready, V)
                dve.wait_ge(conv_ready, V)
                dve.wait_ge(state_kept, V)
                TT(two(ext[:, 2:2 + T]), pair(lin[0]), two(rstd[:, :]), ALU.mult).then_inc(out_free, 1)
                dve.wait_ge(y_ready, V + 1)
                dve.wait_ge(out_free, g + 1)
                if first:
                    dve.wait_ge(sadd_ready, phase)
                w0 = col("ffn_conv_w", l * 3 * FC + it)
                w1 = col("ffn_conv_w", l * 3 * FC + FC + it)
                STT(out=ty[:, 0:SEQ], in0=ext[:, 1:1 + SEQ], scalar=w1, in1=ty[:, 0:SEQ], op0=ALU.mult, op1=ALU.add
                    ).then_inc(ffn_tap, 1)
                TT(ty[:, SEQ:T].unsqueeze(1), ty[:, SEQ:T].unsqueeze(1), sadd[:, ds(it, 1), :], ALU.add
                   ).then_inc(ffn_tap, 1)
                dve.wait_ge(ffn_tap, 2 * (l * FC + it) + 2)
                STT(out=ty[:, 0:SEQ], in0=ext[:, 0:SEQ], scalar=w0, in1=ty[:, 0:SEQ], op0=ALU.mult, op1=ALU.add
                    ).then_inc(conv_ready, 1)
                split_next(seg, it, 1, last)
                dve.wait_ge(unit_done, seg.u0 + 2 * it + 2)
                dve.wait_ge(scaled_ready, l * FC + it + 1)
                dve.wait_ge(z_lo, V)
                TT(two(tt[:, :]), pair(lin[1]), two(tsl[:, :]), ALU.mult).then_inc(out_free, 1)
                z_split(it, V)
            loop(dve, seg.halves, body)

            seg2 = segs[f"dn{l}"]
            n = 2 * l + 2

            def body2(i2, first, last):
                for a in range(2):
                    for p in range(2):
                        if not (last and a == 1):
                            split(seg2.u0 + 4 * i2 + 2 * a + p + 2, p, KH)
                        elif seg2.next_kt:
                            split(seg2.u0 + 4 * i2 + 2 * a + p + 2, p, seg2.next_kt)
                    m = 2 * i2 + a
                    dve.wait_ge(unit_done, seg2.u0 + 4 * i2 + 2 * a + 2)
                    TT(two(at1(x, m)), pair(lin[a]), two(at1(x, m)), ALU.add).then_inc(out_free, 1)
                    if n < NORMS:
                        prep(n, m)
            loop(dve, DC // 2, body2)

        V_.memset(eps[:, :], EPS)
        split(0, 0, 8)
        split(1, 1, 8)
        nfill = -(-NBK // 4)
        for i in range(nfill + 1 + DC):
            dve.wait_ge(filled, i + 1)
            bank = (aux, aux2)[(i % 4) // 2][:, i % 2, :]
            if i < nfill:
                n = min(512, nrows - 512 * i)
                V_.tensor_copy(par[:, 512 * i:512 * i + n], bank[:, 0:n]).then_inc(fill_free, 1)
            elif i == nfill:
                V_.tensor_copy(x[:, :, SEQ:T], bank[:, 0:DC * NS].rearrange("p (c s) -> p c s", c=DC)).then_inc(fill_free, 1)
                dve.wait_ge(fill_free, i + 1)
            else:
                V_.tensor_copy(x[:, i - nfill - 1, 0:SEQ], bank).then_inc(x_in, 1)
        for m in range(DC):
            dve.wait_ge(x_in, m + 1)
            prep(0, m)

        short_conv(0, 0, 0, 1)
        ffn(0, 1, 2)

        def q_ep(m, g, ps):
            TT(two(at1(qT, m)), pair(ps), two(rstd[:, :]), ALU.mult).then_inc(out_free, 1)
        seg_loop(segs["q"], q_ep, norm=2)

        n = [0]

        def lf(ins):
            n[0] += 1
            ins.then_inc(lf_dve, 1)
            dve.wait_ge(lf_dve, n[0])
        dve.wait_ge(rows_out, 16 * rows_dmas[2])
        lf(V_.memset(negc[:, :].bitcast(F32), 0.0))
        dve.wait_ge(lf_pe, 1)
        lf(TT(two(tt[0:NH, :]), pair(aux)[0:NH], two(rstd[0:NH, :]), ALU.mult))
        lf(TS(tt[0:NH, :], tt[0:NH, :], bf[:, 0:1], None, ALU.add))
        lf(STT(out=ty[0:NH, :], in0=tt[0:NH, :], scalar=-1.0, in1=tt[0:NH, :], op0=ALU.mult, op1=ALU.max))
        dve.wait_ge(lf_act, 1)
        lf(TS(tsq[0:NH, :], tsl[0:NH, :], 1.0, None, ALU.add))
        lf(STT(out=tsl[0:NH, :], in0=tsq[0:NH, :], scalar=1.0, in1=tsl[0:NH, :], op0=ALU.subtract, op1=ALU.subtract))
        dve.wait_ge(lf_act, 2)
        lf(V_.reciprocal(tsq[0:NH, :], tsq[0:NH, :]))
        lf(TT(tsl[0:NH, :], tsl[0:NH, :], tsq[0:NH, :], ALU.mult))
        lf(TT(ty[0:NH, :], ty[0:NH, :], tsl[0:NH, :], ALU.subtract))
        lf(STT(out=lfT[:, :], in0=tt[0:NH, :], scalar=0.0, in1=ty[0:NH, :], op0=ALU.min, op1=ALU.subtract))
        lf(V_.tensor_tensor_scan(tt[0:NH, 0:SEQ], ones[0:NH, 0:1].to_broadcast([NH, SEQ]), lfT[:, 0:SEQ], 0.0,
                                 ALU.mult, ALU.add))
        dve.wait_ge(lf_act, 3)
        lf(STT(out=negc[32:32 + NH, :], in0=tt[0:NH, 0:SEQ], scalar=-1.0, in1=negc[0:NH, :].bitcast(F32),
               op0=ALU.mult, op1=ALU.subtract))

        def normalise(i, tile, m, gain):
            dve.wait_ge(head_root, i + 1)
            V_.reciprocal(ty[:, :], ty[:, :]).then_inc(head_recip, 1)
            dve.wait_ge(head_recip, i + 1)
            STT(out=at1(tile, m), in0=at1(tile, m), scalar=gain[:, 0:1], in1=ty[:, :].unsqueeze(1),
                op0=ALU.mult, op1=ALU.mult).then_inc(normed, 1)

        dve.wait_ge(small_landed, 16 * 8)
        V_.tensor_scalar(qg[:, :], qg[:, :], HD ** -0.5, None, ALU.mult).then_inc(lf_dve, 1)
        dve.wait_ge(lf_dve, 13)

        def k_ep(m, g, ps):
            TT(two(at1(kT, m)), pair(ps), two(rstd[:, :]), ALU.mult).then_inc(out_free, 1)
            normalise(m, qT, m, qg)
        seg_loop(segs["k"], k_ep)

        def v_ep(m, g, ps):
            if above_zero(m):
                dve.wait_ge(v_T, m)
            TT(two(tt[:, :]), pair(ps), two(rstd[:, :]), ALU.mult).then_inc(out_free, 1)
            normalise(DC + m, kT, m, kg)
        dve.wait_ge(qh_ready, 1)
        TT(ql[:, :, :], qT[:, :, SEQ:T], qh[:, :, :].bitcast(F32), ALU.subtract).then_inc(ql_ready, 1)
        seg_loop(segs["v"], v_ep)

        dve.wait_ge(normed, 2 * DC)
        TT(qk[:, :, :], qT[:, :, SEQ:T], kT[:, :, SEQ:T], ALU.mult).then_inc(qk_ready, 1)
        V_.memset(sc[:, NPAGES, :], 0.0)
        dve.wait_ge(v_T, DC)
        dve.wait_ge(lf_rows, 1)
        V_.tensor_copy(lftok[:, 0:QB, :], aux[:, 0, 0:QB * NH].rearrange("p (t h) -> p t h", h=NH))
        V_.tensor_copy(lftok[0:NS, QB, :], aux[0:NS, 0, QB * NH:(QB + 1) * NH]).then_inc(lf_rows, 1)
        for half in range(2):
            dve.wait_ge(suffix, half + 1)
            if half == 0:
                dve.wait_ge(suffix, 2)
            V_.tensor_copy(lfb[:, 32 * half:32 * half + 32, :].rearrange("p a h -> p (a h)"),
                           aux[:, 1, :] if half == 0 else lin[0][:, 0, :]).then_inc(suffix_in, 1)

        items = {s + 1: (k, i, m) for m, (s, k, i) in enumerate(B67)}
        for t in range(STEPS + 5):
            if t < STEPS:
                b, h = kv[t]
                w = (b + 1) * P
                dve.wait_ge(s_ready, t + 1)
                V_.reduce_max(nmax[:, t:t + 1], psf["S"][t % 2][:, 0:w], AX.X, negate=True).then_inc(max_ready, 1)
            for g in range(pages_by(t - 1), pages_by(t)):
                ring = (pages, k_pages2)[g // 4 % 2]
                if g % 4 == 3:
                    dve.wait_ge(qb_ready, g // NPG + 1)
                    dve.wait_ge(page_landed[g % 8], 16 * (g // 8 + 1))
                    TT(ring[:, 3, :], ring[:, 3, :], qb[:, g // NPG % 2, :], ALU.mult).then_inc(k_mult3, 1)
                    dve.wait_ge(k_mult3, g // 4 + 1)
                else:
                    dve.wait_ge(k_mult, pool_pages(g + 1))
                V_.reduce_sum(sc[:, g, :], ring[:, g % 4, :].rearrange("p (h d) -> p h d", d=HD), AX.X
                              ).then_inc(k_reduced, 1)
            if t % NH == 3 and t > NH:
                b = (t - 3) // NH - 1
                dve.wait_ge(pv_done, NH * (b + 1))
                if above_zero(b):
                    dve.wait_ge(zT_hi, b)
                V_.reciprocal(rinv[:, :], rsum[:, NH * b:NH * (b + 1)]).then_inc(zt_step, 1)
                dve.wait_ge(zt_step, b + 1)
                for half in range(2):
                    hs = NH // 2
                    TT(ztok[:, half * 512:(half + 1) * 512].rearrange("p (h d) -> p h d", d=HD),
                       aux[:, half, :].rearrange("p (h d) -> p h d", d=HD),
                       rinv[:, half * hs:(half + 1) * hs].unsqueeze(2).to_broadcast([P, hs, HD]), ALU.mult
                       ).then_inc(zt_ready, 1)
            if t in items and items[t][0] == "zT":
                i = items[t][1]
                dve.wait_ge(zT_hi, i + 1)
                TT(hl[:, 0:DC, i * P:(i + 1) * P], flat2(aux2).rearrange("p (c t) -> p c t", c=DC),
                   hh[:, 0:DC, i * P:(i + 1) * P].bitcast(F32), ALU.subtract).then_inc(b67_free, 1)

        n[0] = 0

        def smx(ins):
            n[0] += 1
            ins.then_inc(sm_dve, 1)
            dve.wait_ge(sm_dve, n[0])
        B2, B3 = lin[1][:, 0, :], lin[1][:, 1, :]
        spread = ident[0:NS, 0:NS].unsqueeze(2).to_broadcast([NS, NS, NH])

        def sh(i, n_=P):
            return sm[0:n_, i, :].rearrange("p (s h) -> p s h", h=NH)

        sc4 = sc[:, 0:NPAGES, :].rearrange("p (s g) h -> p s g h", g=NPG)

        dve.wait_ge(pv_done, STEPS)
        dve.wait_ge(sm_pe, 1)
        smx(TT(sh(1, NS), B2[0:NS, 0:NH].unsqueeze(1).to_broadcast([NS, NS, NH]), spread, ALU.mult))
        smx(TT(sh(2, NS), lftok[0:NS, QB, :].unsqueeze(1).to_broadcast([NS, NS, NH]), spread, ALU.mult))
        dve.wait_ge(sm_pe, 2)
        smx(TT(sc[:, 0:NPAGES, :], sc[:, 0:NPAGES, :], lfb[:, :, :], ALU.add))
        for s in range(NS):
            ins = TT(sc4[:, s], sc4[:, s], B2[:, 2 * P + s * NH:2 * P + (s + 1) * NH].unsqueeze(1).to_broadcast([P, NPG, NH]),
                     ALU.add)
        smx(ins)
        smx(V_.tensor_reduce(sh(3), sc[:, 0:NPAGES, :].rearrange("p (s g) h -> p s h g", g=NPG), AX.X, ALU.max))
        smx(TT(sm[:, 3, :], sm[:, 3, :], B2[:, P:2 * P], ALU.max))
        dve.wait_ge(sm_pe, 3)
        smx(V_.reduce_max(smal[:, 0:1], B3[:, 0:P], AX.X))
        smx(TS(sm[:, 5, :], ident[:, :], smal[:, 0:1], None, ALU.mult))
        smx(V_.tensor_copy(sm[:, 4, :], B2[:, P:2 * P]))
        dve.wait_ge(sm_pe, 4)
        smx(TT(sm[:, 4, :], sm[:, 4, :], B3[:, P:2 * P], ALU.subtract))
        for s in range(NS):
            ins = TT(sc4[:, s], sc4[:, s], B3[:, P + s * NH:P + (s + 1) * NH].unsqueeze(1).to_broadcast([P, NPG, NH]),
                     ALU.subtract)
        smx(ins)
        dve.wait_ge(sm_act, 2)
        smx(V_.tensor_reduce(sh(5), sc[:, 0:NPAGES, :].rearrange("p (s g) h -> p s h g", g=NPG), AX.X, ALU.add))
        smx(STT(out=sm[:, 5, :], in0=sm[:, 4, :], scalar=1.0 / P, in1=sm[:, 5, :], op0=ALU.mult, op1=ALU.add))
        dve.wait_ge(sm_pe, 5)
        smx(V_.reciprocal(sm[:, 0, :], B3[:, 2 * P:3 * P]))
        for s in range(NS):
            ins = TT(sc4[:, s], sc4[:, s], sm[:, 0, s * NH:(s + 1) * NH].unsqueeze(1).to_broadcast([P, NPG, NH]), ALU.mult)
        smx(ins)
        smx(TT(sm[:, 4, :], sm[:, 4, :], sm[:, 0, :], ALU.mult))
        smx(TT(sh(3, NS), sh(4, NS), spread, ALU.mult))
        split(segs["wo"].u0, 0, 8)
        split(segs["wo"].u0 + 1, 1, 8)
        for half in range(2):
            dve.wait_ge(v_sum, half + 1)
            if above_zero(half):
                dve.wait_ge(o_T, half)
            TT(osb[:, :].rearrange("p (h d) -> p h d", d=HD), flat2((aux, aux2)[half]).rearrange("p (h d) -> p h d", d=HD),
               head_mask[:, :].unsqueeze(2).to_broadcast([P, NH, HD]), ALU.mult).then_inc(osb_ready, 1)
            dve.wait_ge(o_hi, half + 1)
            TT(hl[:, 0:DC, SEQ + 4 * half:SEQ + 4 * half + 4],
               B2[:, 384 + 32 * half:416 + 32 * half].rearrange("p (c s) -> p c s", c=DC),
               hh[:, 0:DC, SEQ + 4 * half:SEQ + 4 * half + 4].bitcast(F32), ALU.subtract).then_inc(zs_ready, 1)
        out_proj("wo", 3)
        ffn(1, 2, 3)

        n[0] = 0

        def ls(ins):
            n[0] += 1
            ins.then_inc(lsp_dve, 1)
            dve.wait_ge(lsp_dve, n[0])
        lam = par[:, rows["lru_lambda"]:rows["lru_lambda"] + LC]
        ls(TS(lsp[:, 0, :], lam, -1.0, 0.0, ALU.mult, ALU.max))
        ls(STT(out=lsp[:, 1, :], in0=lam, scalar=-1.0, in1=lam, op0=ALU.mult, op1=ALU.max))
        dve.wait_ge(lsp_act, 1)
        ls(TS(lsp[:, 3, :], lsp[:, 2, :], 1.0, None, ALU.add))
        ls(STT(out=lsp[:, 5, :], in0=lsp[:, 3, :], scalar=1.0, in1=lsp[:, 2, :], op0=ALU.subtract, op1=ALU.subtract))
        ls(V_.reciprocal(lsp[:, 6, :], lsp[:, 3, :]))
        ls(TT(lsp[:, 5, :], lsp[:, 5, :], lsp[:, 6, :], ALU.mult))
        dve.wait_ge(lsp_act, 2)
        ls(TT(lsp[:, 5, :], lsp[:, 4, :], lsp[:, 5, :], ALU.subtract))
        ls(TT(lsp[:, 7, :], lsp[:, 5, :], lsp[:, 0, :], ALU.add))
        ls(TS(lsp[:, 7, :], lsp[:, 7, :], -LRU_C, None, ALU.mult))
        pads(3, 4)

        v0 = conv0["lru"]

        def lx_evacuate(m, ps):
            if isinstance(m, int) and m == 0:
                dve.wait_ge(sadd_ready, 4)
            if above_zero(m):
                dve.wait_ge(xb_ready, m)
            TT(two(tt[:, :]), pair(ps), two(rstd[:, :]), ALU.mult).then_inc(out_free, 1)

        def lx_ep(m, g, ps):
            V = v0 + m
            dve.wait_ge(y_ready, V + 1)
            w0, w1, w2 = (col("lru_conv_w", k * LC + m) for k in range(3))
            STT(out=ty[:, 0:SEQ], in0=ext[:, 2:2 + SEQ], scalar=w2, in1=ty[:, 0:SEQ], op0=ALU.mult, op1=ALU.add
                ).then_inc(lru_tap, 1)
            TT(xc[:, ds(m, 1), SEQ:T], ty[:, SEQ:T].unsqueeze(1), sadd[:, ds(m, 1), :], ALU.add).then_inc(lru_tap, 1)
            dve.wait_ge(lru_tap, 3 * m + 2)
            STT(out=ty[:, 0:SEQ], in0=ext[:, 1:1 + SEQ], scalar=w1, in1=ty[:, 0:SEQ], op0=ALU.mult, op1=ALU.add
                ).then_inc(lru_tap, 1)
            dve.wait_ge(lru_tap, 3 * m + 3)
            STT(out=xc[:, ds(m, 1), 0:SEQ], in0=ext[:, 0:SEQ].unsqueeze(1), scalar=w0, in1=ty[:, 0:SEQ].unsqueeze(1),
                op0=ALU.mult, op1=ALU.add).then_inc(conv_ready, 1)
        seg_loop(segs["lx"], lx_ep, norm=4, evacuate=lx_evacuate)

        def expm1(m):
            dve.wait_ge(lru_ex, m + 1)
            if m:
                dve.wait_ge(lru_q, m)
            TT(tsl[:, :], la[:, m % 5, :], la[:, m % 5, :], ALU.mult).then_inc(lru_sq, 1)
            dve.wait_ge(lru_sq, m + 1)
            STT(out=gate[:, m, :], in0=tsl[:, :], scalar=1.0, in1=gate[:, m, :], op0=ALU.add, op1=ALU.mult).then_inc(lru_q, 1)

        def scan(m):
            h0 = rows["state_lru_h"]
            dve.wait_ge(lru_b, m + 1)
            if m:
                dve.wait_ge(lru_h, m)
            TT(stmp[:, 0, :], la[:, m % 5, SEQ:T], par[:, h0 + m:h0 + m + (NS - 1) * LC + 1:LC], ALU.mult).then_inc(lru_s, 1)
            dve.wait_ge(lru_s, m + 1)
            TT(xc[:, m, SEQ:T], lb[:, m % 5, SEQ:T], stmp[:, 0, :], ALU.add)
            V_.tensor_tensor_scan(xc[:, m, 0:SEQ], la[:, m % 5, 0:SEQ], lb[:, m % 5, 0:SEQ], 0.0, ALU.mult, ALU.add
                                  ).then_inc(lru_h, 1)

        def z_mult(m):
            dve.wait_ge(lru_h, m + 1)
            dve.wait_ge(gelu_ready, m + 1)
            dve.wait_ge(z_lo, v0 + m)
            TT(tz[:, :], xc[:, m, :], gate[:, m, :], ALU.mult).then_inc(lru_zt, 1)

        def z_low(m):
            dve.wait_ge(z_hi, v0 + m + 1)
            dve.wait_ge(h_kept, m + 1)
            TT(hl[:, m, :], tz[:, :], hh[:, m, :].bitcast(F32), ALU.subtract).then_inc(z_lo, 1)

        def gate_branch(name, first_m, scans):
            seg = segs[name]
            for i in range(seg.units):
                m = first_m + i
                split_next(seg, i // 2, i % 2, i // 2 == seg.halves - 1)
                if m:
                    z_mult(m - 1)
                if m in scans:
                    scan(m)
                dve.wait_ge(unit_done, seg.u0 + i + 1)
                if m:
                    dve.wait_ge(gelu_ready, m)
                else:
                    dve.wait_ge(xb_ready, LC)
                TT(two(tt[:, :]), pair(lin[i % 2]), two(rstd[:, :]), ALU.mult).then_inc(out_free, 1)
                if m:
                    z_low(m - 1)

        for m in range(5):
            expm1(m)
        gate_branch("lgA", 0, range(0, LGA))
        for m in range(LGA, 5):
            scan(m)
        for m in range(5, LC):
            expm1(m)
        gate_branch("lgB", LGA, range(5, LC))
        z_mult(LC - 1)
        z_low(LC - 1)
        out_proj("lo", 5)
        ffn(2, 4, 5)
        short_conv(1, 6, 5, 6)
        ffn(3, 6, 7)

    @block.gpsimd
    def _(pool):
        G = nc.gpsimd
        TT = G.tensor_tensor

        steps = [0]

        def link(ins):
            steps[0] += 1
            ins.then_inc(sadd_step, 1)
            pool.wait_ge(sadd_step, steps[0])
        for tile in (ones, ident, blk, jsel):
            link(G.memset(tile[:, :], 1.0 if tile is ones else 0.0))
        link(G.memset(tz[:, 0:P], 0.0))
        link(G.memset(tz[:, P:P + 2 * NH], 0.0))
        link(G.memset(head_mask[:, :], 0.0))
        link(G.affine_select(out=tri[:, :], in_=ones[:, :], compare_op=ALU.is_gt, fill=0.0, base=0, pattern=[[-1, P]],
                             channel_multiplier=1))
        link(G.memset(blk[0:HD, 0:HD], 1.0))
        link(G.memset(blk[HD:P, HD:P], 1.0))
        for j in range(4):
            link(G.memset(jsel[32 * j:32 * j + 32, j:j + 1], 1.0))
        link(G.affine_select(out=tz[:, 0:P], in_=tz[:, 0:P], compare_op=ALU.is_ge, fill=MASK_VALUE, base=0, pattern=[[-1, P]],
                             channel_multiplier=1))
        for base in (0, -32, -64, -96):
            link(G.affine_select(out=head_mask[:, :], in_=head_mask[:, :], compare_op=ALU.not_equal, fill=1.0, base=base,
                                 pattern=[[-1, NH]], channel_multiplier=1))
        for at_, fill in ((P, 1.0), (P + NH, -1.0)):
            for base in (0, -32):
                link(G.affine_select(out=tz[:, at_:at_ + NH], in_=tz[:, at_:at_ + NH], compare_op=ALU.not_equal, fill=fill,
                                     base=base, pattern=[[-1, NH]], channel_multiplier=1))
        link(G.affine_select(out=ident[:, :], in_=ident[:, :], compare_op=ALU.not_equal, fill=1.0, base=0, pattern=[[-1, P]],
                             channel_multiplier=1))
        G.memset(acc[:, :], 0.0).then_inc(acc_ready, 1)
        G.tensor_copy(identr[:, :], ident[:, :]).then_inc(consts, 1)
        G.tensor_copy(maskr[:, :], tz[:, 0:P]).then_inc(consts, 1)
        G.tensor_copy(pickm[:, :], tz[:, P + NH:P + 2 * NH])
        G.tensor_copy(pick[:, :], tz[:, P:P + NH]).then_inc(consts, 1)

        def prep(n, m, p):
            pool.wait_ge(sq_ready, DC * n + m + 1)
            pool.wait_ge(acc_ready, 9 * n + 1 + m)
            TT(acc[:, :], acc[:, :], squares[p][:, :], ALU.add).then_inc(acc_ready, 1)

        def reset(n):
            pool.wait_ge(ssq_ready, n + 1)
            G.memset(acc[:, :], 0.0).then_inc(acc_ready, 1)
            pool.wait_ge(rstd_ready, n + 1)

        def sample_add(weights, state, chunks, taps, lay, s_stride, phase):
            r0, w0 = rows[state] + lay * NS * s_stride, rows[weights] + lay * (taps + 1) * chunks
            old = par[:, r0:r0 + NS * s_stride].rearrange("p (s k c) -> p k c s", s=NS, k=taps)
            if above_zero(phase - 1):
                pool.wait_ge(sadd_ready, phase - 1)
            for k in range(taps):
                w = par[:, w0 + k * chunks:w0 + (k + 1) * chunks].unsqueeze(2).to_broadcast([P, chunks, NS])
                dst = sadd if k == 0 else stmp
                link(TT(dst[:, 0:chunks, :], old[:, k], w, ALU.mult))
                if k == taps - 1:
                    TT(sadd[:, 0:chunks, :], sadd[:, 0:chunks, :], stmp[:, 0:chunks, :], ALU.add).then_inc(sadd_ready, 1)
                elif k:
                    link(TT(sadd[:, 0:chunks, :], sadd[:, 0:chunks, :], stmp[:, 0:chunks, :], ALU.add))

        def chunk_sum(n):
            with pool.Fori(0, DC // 2) as i:
                for p in range(2):
                    prep(n, 2 * i + p, p)

        def keep(m, q, chunks):
            G.tensor_copy(sto[:, 0:q * chunks].rearrange("p (q c) -> p q c", c=chunks)[:, :, ds(m, 1)],
                          ext[:, SEQ:SEQ + q].unsqueeze(2)).then_inc(state_kept, 1)

        def short_conv(j, n, which, phase):
            v0 = conv0[f"sc{j}"]
            if above_zero(which):
                pool.wait_ge(rows_T, which)
            sample_add("sc_conv_w", "state_sconv", DC, 2, j, 2 * DC, phase)
            reset(n)
            with pool.Fori(0, DC) as m:
                pool.wait_ge(out_free, segs[f"c{j}"].g0 + m + 1)
                TT(at1(cst, m), at1(cst, m), rstd[:, :].unsqueeze(1), ALU.mult).then_inc(c_scaled, 1)
            with pool.Fori(0, DC) as m:
                pool.wait_ge(out_free, segs[f"h{j}"].g0 + m + 1)
                keep(m, 10, DC)
                pool.wait_ge(conv_ready, v0 + m + 1)
                TT(at1(cst, m), at1(cst, m), rstd[:, :].unsqueeze(1), ALU.mult).then_inc(conv_scaled, 1)
            chunk_sum(n + 1)

        def ffn(l, which, phase):
            seg, v0 = segs[f"gu{l}"], conv0[f"ffn{l}"]
            pool.wait_ge(rows_T, which)
            sample_add("ffn_conv_w", "state_ffn_conv", FC, 2, l, 2 * FC, phase)
            reset(2 * l + 1)
            with pool.Fori(0, FC) as it:
                pool.wait_ge(out_free, seg.g0 + 2 * it + 1)
                keep(it, 10, FC)
                pool.wait_ge(silu_ready, l * FC + it + 1)
                TT(tsl[:, :], tsl[:, :], rstd[:, :], ALU.mult).then_inc(scaled_ready, 1)
            if 2 * l + 2 < NORMS:
                chunk_sum(2 * l + 2)

        pool.dma_start(pt[:, :], I["page_table"].rearrange("(o s) g -> o (s g)", o=1)).then_inc(small_landed, 16)
        pool.dma_start(bf[:, :], I["fox_b_f"].rearrange("o h -> h o")).then_inc(small_landed, 16)
        for dst, src in ((qg, I["fox_q_norm"]), (kg, I["fox_k_norm"])):
            for r in (0, HD):
                pool.dma_start(dst[r:r + HD, :], src.rearrange("o h -> h o")).then_inc(small_landed, 16)
        pool.dma_start(wf[:, :, :], I["fox_w_f"][0].rearrange("(k p) h -> p k h", p=P)).then_inc(small_landed, 16)
        pool.dma_start(O["new_sconv_sample"][:, :, 0, :], I["state_sconv"][:, :, 1, :]).then_inc(small_landed, 16)
        pool.dma_start(O["new_ffn_conv_sample"][:, :, 0, :], I["state_ffn_conv"][:, :, 1, :]).then_inc(copies, 16)
        pool.dma_start(O["new_lru_conv_sample"][:, :, 0:2, :], I["state_lru_conv"][:, :, 1:3, :]).then_inc(copies, 16)
        pool.wait_ge(fill_free, -(-NBK // 4))
        chunk_sum(0)
        short_conv(0, 0, 0, 1)
        ffn(0, 1, 2)

        reset(2)
        pool.wait_ge(unit_done, segs["dn0"].u0 + 16)
        pool.wait_ge(small_landed, 16 * 8)
        with pool.Fori(0, NS * NPG) as i:
            idx = pool.value_load(pt[0:1, ds(i, 1)], min_val=0, max_val=NPOOL - 1)
            pool.dma_start(lfb[:, ds(i, 1), :], I["cache_logf"][0][ds(idx, 1)].rearrange("a p h -> p a h")
                           ).then_inc(lf_landed, 16)
        with pool.Fori(0, NS // 2) as i:
            for s in range(2):
                for g in range(NPG):
                    n = s * NPG + g
                    if g == 0:
                        pool.wait_ge(qb_ready, 2 * i + s + 1)
                    if n % 4 == 3:
                        continue
                    pool.wait_ge(page_landed[n % 8], 32 * i + 16 * (n // 8 + 1))
                    ring = (pages, k_pages2)[n // 4 % 2]
                    TT(ring[:, n % 4, :], ring[:, n % 4, :], qb[:, s, :], ALU.mult).then_inc(k_mult, 1)
        chunk_sum(3)
        ffn(1, 2, 3)

        v0 = conv0["lru"]
        pool.wait_ge(rows_T, 3)
        pool.wait_ge(unit_done, segs["dn1"].u0 + 16)
        for b in band.values():
            G.memset(b[:, :], 0.0).then_inc(band_zero, 1)
        sample_add("lru_conv_w", "state_lru_conv", LC, 3, 0, 3 * LC, 4)
        reset(4)
        with pool.Fori(0, LC) as m:
            pool.wait_ge(xb_ready, m + 1)
            keep(m, 11, LC)
        for hf in range(2):
            ms = range(5 * hf, 5 * hf + 5)
            for m in ms:
                pool.wait_ge(out_free, segs[f"gates{hf}"].g0 + 2 * (m % 5) + 2)
                TT(lb[:, m % 5, :], lb[:, m % 5, :], xc[:, m, :], ALU.mult).then_inc(lru_ix, 1)
            for m in ms:
                pool.wait_ge(lru_root, m + 1)
                TT(lb[:, m % 5, :], lb[:, m % 5, :], xc[:, m, :], ALU.mult).then_inc(lru_b, 1)
            for m in ms:
                pool.wait_ge(lru_h, m + 1)
                G.tensor_copy(hst[:, :, m], xc[:, m, SEQ - 1:T]).then_inc(h_kept, 1)
        chunk_sum(5)
        ffn(2, 4, 5)
        short_conv(1, 6, 5, 6)
        ffn(3, 6, 7)

    psum.close()


def _outs(i):
    B, SEQ, D = i["x_prompt"].shape
    S_ = i["x_sample"].shape[0]
    NA, _, r, _ = i["state_sconv"].shape
    NB, _, _, H, HDIM = i["cache_k"].shape
    NC, _, LW = i["state_lru_h"].shape
    rl = i["state_lru_conv"].shape[2]
    DEPTH, _, rf, F = i["state_ffn_conv"].shape
    return [("y_prompt", (B, SEQ, D)), ("y_sample", (S_, 1, D)),
            ("new_sconv_prompt", (NA, B, r, D)), ("new_sconv_sample", (NA, S_, r, D)),
            ("new_k_prompt", (NB, B, SEQ, H, HDIM)), ("new_v_prompt", (NB, B, SEQ, H, HDIM)), ("new_logf_prompt", (NB, B, SEQ, H)),
            ("new_k_sample", (NB, S_, 1, H, HDIM)), ("new_v_sample", (NB, S_, 1, H, HDIM)), ("new_logf_sample", (NB, S_, 1, H)),
            ("new_lru_h_prompt", (NC, B, LW)), ("new_lru_h_sample", (NC, S_, LW)),
            ("new_lru_conv_prompt", (NC, B, rl, LW)), ("new_lru_conv_sample", (NC, S_, rl, LW)),
            ("new_ffn_conv_prompt", (DEPTH, B, rf, F)), ("new_ffn_conv_sample", (DEPTH, S_, rf, F))]


def kernel(**inputs):
    import numpy as np
    import concourse.bacc as bacc
    from concourse.bass_utils import run_bass_kernel_spmd

    nc = bacc.Bacc("TRN2", target_bir_lowering=False, num_devices=1)
    arrays = {name: np.ascontiguousarray(a) for name, a in inputs.items()}
    ins = {name: nc.dram_tensor(name, a.shape, mybir.dt.from_np(a.dtype), kind="ExternalInput").ap()
           for name, a in arrays.items()}
    outs = {name: nc.dram_tensor(name, shape, F32, kind="ExternalOutput").ap() for name, shape in _outs(arrays)}
    hybrid_step(nc, ins, outs)
    result = run_bass_kernel_spmd(nc, [arrays], core_ids=[0]).results[0]
    return tuple(result[name] for name, _ in _outs(arrays))
```
